# Optimizing a Trainium2 kernel written in Bass

```python
import math
import jax, jax.numpy as jnp
from jax import lax
import numpy as np

D_MODEL = 1024
BATCH = 1
SEQ = 512
DEPTH = 1

N_META = 16
ATT_HEADS = 4
ATT_HEAD_DIM = 64
ATT_V_DIM = 2 * ATT_HEAD_DIM
REC_HEADS = 4
REC_DK = 128
REC_DV = 128
ATT_WIDTH = ATT_HEADS * ATT_V_DIM
REC_WIDTH = REC_HEADS * REC_DV
MIX_WIDTH = ATT_WIDTH + REC_WIDTH
COL_SIZES = (
    ATT_HEADS * 2 * ATT_HEAD_DIM,
    ATT_HEADS * 2 * ATT_HEAD_DIM,
    ATT_WIDTH,
    REC_HEADS * REC_DK,
    REC_HEADS * REC_DK,
    REC_WIDTH,
    REC_WIDTH,
)
IN_COLS = sum(COL_SIZES)
SPLIT_POINTS = tuple(int(v) for v in np.cumsum(COL_SIZES)[:-1])
Q_BLOCK = 128
REC_CHUNK = 64
ROPE_THETA = 10000.0
PEER_HEADS = 8
PEER_QUERY_DIM = 256
N_KEYS = 128
N_EXPERTS = N_KEYS * N_KEYS
PEER_TOPK = 16
PEER_BLOCK = 128
EPS = 1e-6


def rmsnorm(x, w):
    xf = x.astype(jnp.float32)
    y = xf * lax.rsqrt(jnp.mean(xf * xf, axis=-1, keepdims=True) + EPS)
    return (y * w.astype(jnp.float32)).astype(x.dtype)

def rope_tables(T, d):
    inv_freq = ROPE_THETA ** (-jnp.arange(0, d, 2, dtype=jnp.float32) / d)
    ang = jnp.arange(T, dtype=jnp.float32)[:, None] * inv_freq[None, :]
    ang = jnp.concatenate([ang, ang], axis=-1)
    return jnp.cos(ang), jnp.sin(ang)

def apply_rope(z, cos, sin):
    half = z.shape[-1] // 2
    rot = jnp.concatenate([-z[..., half:], z[..., :half]], axis=-1)
    return (z * cos.astype(z.dtype) + rot * sin.astype(z.dtype)).astype(z.dtype)

def lambda_init(layer_idx):
    return 0.8 - 0.6 * math.exp(-0.3 * layer_idx)

def diff_attention(aq, ak, av, lq1, lk1, lq2, lk2, subln_w, lam_init, cos, sin):
    B, T, _ = aq.shape
    q = apply_rope(aq.reshape(B, T, ATT_HEADS, 2, ATT_HEAD_DIM).transpose(3, 0, 2, 1, 4), cos, sin)
    k = apply_rope(ak.reshape(B, T, ATT_HEADS, 2, ATT_HEAD_DIM).transpose(3, 0, 2, 1, 4), cos, sin)
    v = av.reshape(B, T, ATT_HEADS, ATT_V_DIM).transpose(0, 2, 1, 3)
    q = q * (ATT_HEAD_DIM ** -0.5)
    lam = (jnp.exp(jnp.sum(lq1.astype(jnp.float32) * lk1.astype(jnp.float32)))
           - jnp.exp(jnp.sum(lq2.astype(jnp.float32) * lk2.astype(jnp.float32))) + lam_init)
    neg = jnp.finfo(jnp.float32).min

    def block(q_blk, k_blk, v_blk, q_start):
        nq, nk = q_blk.shape[-2], k_blk.shape[-2]
        mask = jnp.arange(nk)[None, :] <= (q_start + jnp.arange(nq))[:, None]
        s = jnp.einsum('pbhqd,pbhkd->pbhqk', q_blk, k_blk).astype(jnp.float32)
        p = jax.nn.softmax(jnp.where(mask, s, neg), axis=-1)
        w = p[0] - lam * p[1]
        return jnp.einsum('bhqk,bhkv->bhqv', w.astype(v_blk.dtype), v_blk)

    outs = [block(q[..., :N_META, :], k[..., :N_META, :], v[:, :, :N_META], 0)]
    for i in range((T - N_META) // Q_BLOCK):
        s0 = N_META + i * Q_BLOCK
        e0 = s0 + Q_BLOCK
        outs.append(block(q[..., s0:e0, :], k[..., :e0, :], v[:, :, :e0], s0))
    o = jnp.concatenate(outs, axis=2)
    o = rmsnorm(o, subln_w) * (1.0 - lam_init)
    return o.transpose(0, 2, 1, 3).reshape(B, T, ATT_WIDTH)

def gla_chunk(S, q, k, v, g):
    C = q.shape[2]
    cum = jnp.cumsum(g, axis=2)
    inter = jnp.einsum('bhtc,bhcv->bhtv', q * jnp.exp(cum), S)
    causal = jnp.tril(jnp.ones((C, C), dtype=bool))[:, :, None]
    diff = cum[:, :, :, None, :] - cum[:, :, None, :, :]
    decay = jnp.where(causal, jnp.exp(jnp.where(causal, diff, 0.0)), 0.0)
    A = jnp.einsum('bhtc,bhsc,bhtsc->bhts', q, k, decay)
    intra = jnp.einsum('bhts,bhsv->bhtv', A, v)
    last = cum[:, :, -1]
    S_new = (jnp.exp(last)[..., None] * S
             + jnp.einsum('bhsc,bhsv->bhcv', k * jnp.exp(last[:, :, None, :] - cum), v))
    return S_new, inter + intra

def hgrn2(rq, rf, ri, rg, lb, norm_w):
    B, T, _ = rq.shape

    def heads(z, d):
        return z.reshape(B, T, REC_HEADS, d).transpose(0, 2, 1, 3).astype(jnp.float32)

    q = jax.nn.silu(heads(rq, REC_DK))
    lbh = lb.reshape(REC_HEADS, 1, REC_DK)
    f = lbh + (1.0 - lbh) * jax.nn.sigmoid(heads(rf, REC_DK))
    k = 1.0 - f
    g = jnp.log(f)
    v = heads(ri, REC_DV)
    S0 = jnp.zeros((B, REC_HEADS, REC_DK, REC_DV), jnp.float32)
    S_meta, o_meta = gla_chunk(S0, q[:, :, :N_META], k[:, :, :N_META], v[:, :, :N_META], g[:, :, :N_META])
    n_chunks = (T - N_META) // REC_CHUNK

    def to_chunks(z):
        z = z[:, :, N_META:].reshape(B, REC_HEADS, n_chunks, REC_CHUNK, z.shape[-1])
        return z.transpose(2, 0, 1, 3, 4)

    _, o_real = lax.scan(lambda S, xs: gla_chunk(S, *xs), S_meta,
                         (to_chunks(q), to_chunks(k), to_chunks(v), to_chunks(g)))
    o_real = o_real.transpose(1, 2, 0, 3, 4).reshape(B, REC_HEADS, T - N_META, REC_DV)
    o = jnp.concatenate([o_meta, o_real], axis=2)
    o = rmsnorm(o, norm_w[:, None, :])
    o = o.transpose(0, 2, 1, 3).reshape(B, T, REC_WIDTH) * jax.nn.silu(rg.astype(jnp.float32))
    return o.astype(rq.dtype)

def token_mix(a, w_in, lb, rec_norm_w, lq1, lk1, lq2, lk2, subln_w, w_out, lam_init, cos, sin):
    proj = jnp.einsum('btd,dc->btc', a, w_in)
    aq, ak, av, rq, rf, ri, rg = jnp.split(proj, SPLIT_POINTS, axis=-1)
    att = diff_attention(aq, ak, av, lq1, lk1, lq2, lk2, subln_w, lam_init, cos, sin)
    rec = hgrn2(rq, rf, ri, rg, lb, rec_norm_w)
    mixed = jnp.concatenate([att, rec.astype(att.dtype)], axis=-1)
    return jnp.einsum('btc,cd->btd', mixed, w_out)

def peer_ffn(h, w_query, subkeys, u_table, v_table):
    B, T, D = h.shape
    n = B * T
    pad = (-n) % PEER_BLOCK
    blocks = jnp.pad(h.reshape(n, D), ((0, pad), (0, 0))).reshape(-1, PEER_BLOCK, D)

    def one_block(xb):
        q = jnp.einsum('nd,dc->nc', xb, w_query).reshape(PEER_BLOCK, PEER_HEADS, 2, PEER_QUERY_DIM // 2)
        s = jnp.einsum('nhpc,hpkc->nhpk', q, subkeys).astype(jnp.float32)
        sv, si = lax.top_k(s, PEER_TOPK)
        cand_s = (sv[:, :, 0, :, None] + sv[:, :, 1, None, :]).reshape(PEER_BLOCK, PEER_HEADS, PEER_TOPK * PEER_TOPK)
        cand_i = (si[:, :, 0, :, None] * N_KEYS + si[:, :, 1, None, :]).reshape(PEER_BLOCK, PEER_HEADS, PEER_TOPK * PEER_TOPK)
        top_s, pos = lax.top_k(cand_s, PEER_TOPK)
        experts = jnp.take_along_axis(cand_i, pos, axis=-1).reshape(PEER_BLOCK, PEER_HEADS * PEER_TOPK)
        gates = jax.nn.softmax(top_s, axis=-1).reshape(PEER_BLOCK, PEER_HEADS * PEER_TOPK)
        u = u_table[experts]
        hid = jax.nn.gelu(jnp.einsum('nkd,nd->nk', u, xb).astype(jnp.float32), approximate=False) * gates
        return jnp.einsum('nk,nkd->nd', hid.astype(xb.dtype), v_table[experts])

    y = lax.map(one_block, blocks).reshape(-1, D)[:n]
    return y.reshape(B, T, D)

def first_inputs(seed: int = 0) -> dict:
    key = jax.random.key(seed)
    ks = jax.random.split(key, 18)
    nrm = jax.random.normal
    f32 = jnp.float32
    return {
        "x": nrm(ks[0], (BATCH, SEQ, D_MODEL), f32),
        "meta_tokens": nrm(ks[1], (N_META, D_MODEL), f32),
        "mix_norm_w": 1.0 + 0.02 * nrm(ks[2], (DEPTH, D_MODEL), f32),
        "w_in": nrm(ks[3], (DEPTH, D_MODEL, IN_COLS), f32) * D_MODEL ** -0.5,
        "rec_lb_logits": 0.5 * nrm(ks[4], (DEPTH + 1, REC_HEADS * REC_DK), f32),
        "rec_norm_w": 1.0 + 0.02 * nrm(ks[5], (DEPTH, REC_HEADS, REC_DV), f32),
        "diff_lambda_q1": 0.1 * nrm(ks[6], (DEPTH, ATT_HEAD_DIM), f32),
        "diff_lambda_k1": 0.1 * nrm(ks[7], (DEPTH, ATT_HEAD_DIM), f32),
        "diff_lambda_q2": 0.1 * nrm(ks[8], (DEPTH, ATT_HEAD_DIM), f32),
        "diff_lambda_k2": 0.1 * nrm(ks[9], (DEPTH, ATT_HEAD_DIM), f32),
        "diff_subln_w": 1.0 + 0.02 * nrm(ks[10], (DEPTH, ATT_V_DIM), f32),
        "w_out": nrm(ks[11], (DEPTH, MIX_WIDTH, D_MODEL), f32) * MIX_WIDTH ** -0.5,
        "ffn_norm_w": 1.0 + 0.02 * nrm(ks[12], (DEPTH, D_MODEL), f32),
        "peer_w_query": nrm(ks[13], (DEPTH, D_MODEL, PEER_HEADS * PEER_QUERY_DIM), f32) * D_MODEL ** -0.5,
        "peer_subkeys": nrm(ks[14], (DEPTH, PEER_HEADS, 2, N_KEYS, PEER_QUERY_DIM // 2), f32) * (PEER_QUERY_DIM // 2) ** -0.5,
        "peer_u": nrm(ks[15], (DEPTH, N_EXPERTS, D_MODEL), f32) * D_MODEL ** -0.5,
        "peer_v": nrm(ks[16], (DEPTH, N_EXPERTS, D_MODEL), f32) * PEER_HEADS ** -0.5,
        "final_norm_w": 1.0 + 0.02 * nrm(ks[17], (D_MODEL,), f32),
    }

def first_block(x, meta_tokens, mix_norm_w, w_in, rec_lb_logits, rec_norm_w,
              diff_lambda_q1, diff_lambda_k1, diff_lambda_q2, diff_lambda_k2,
              diff_subln_w, w_out, ffn_norm_w, peer_w_query, peer_subkeys,
              peer_u, peer_v, final_norm_w):
    B = x.shape[0]
    T = N_META + x.shape[1]
    meta = jnp.broadcast_to(meta_tokens[None].astype(x.dtype), (B, N_META, D_MODEL))
    h = jnp.concatenate([meta, x], axis=1)
    cos, sin = rope_tables(T, ATT_HEAD_DIM)
    lb_all = jnp.cumsum(jax.nn.softmax(rec_lb_logits.astype(jnp.float32), axis=0), axis=0)
    for l in range(DEPTH):
        a = rmsnorm(h, mix_norm_w[l])
        h = h + token_mix(a, w_in[l], lb_all[l], rec_norm_w[l],
                          diff_lambda_q1[l], diff_lambda_k1[l], diff_lambda_q2[l], diff_lambda_k2[l],
                          diff_subln_w[l], w_out[l], lambda_init(l), cos, sin).astype(h.dtype)
        if l == DEPTH - 1:
            h = h[:, N_META:]
        h = h + peer_ffn(rmsnorm(h, ffn_norm_w[l]), peer_w_query[l], peer_subkeys[l],
                         peer_u[l], peer_v[l]).astype(h.dtype)
    return rmsnorm(h, final_norm_w)


DEPTH_2 = 4

N_MIXERS = 3
EXPAND = 2
D_INNER = EXPAND * D_MODEL
POOL_WINDOWS = (2, 4, 8, 16)
N_POOL_GROUPS = len(POOL_WINDOWS)
POOL_GROUP = D_INNER // N_POOL_GROUPS
CONV_WIDTH = 3
N_HEADS = 16
QK_NOPE_DIM = 128
QK_ROPE_DIM = 64
V_HEAD_DIM = D_INNER // N_HEADS
Q_LORA_RANK = 384
KV_LORA_RANK = 256
MLA_IN_DIM = Q_LORA_RANK + KV_LORA_RANK + QK_ROPE_DIM + D_INNER
ATTN_SCALE = (QK_NOPE_DIM + QK_ROPE_DIM) ** -0.5
ROPE_BASE = 10000.0
NORM_EPS = 1e-6
MAX_POS_OFFSET = 1024
N_POOL = (DEPTH_2 + 2) // 3
N_CONV = (DEPTH_2 + 1) // 3
N_MLA = DEPTH_2 // 3


def rms_norm(x, g):
    xf = x.astype(jnp.float32)
    y = xf * lax.rsqrt(jnp.mean(xf * xf, axis=-1, keepdims=True) + NORM_EPS)
    return (y * g.astype(jnp.float32)).astype(x.dtype)

def pool_mixer(xn, w_in, w_grp, scale, w_out):
    B, S, _ = xn.shape
    u, z = jnp.split(xn @ w_in, 2, axis=-1)
    uf = u.astype(jnp.float32).reshape(B, S, N_POOL_GROUPS, POOL_GROUP)
    cs = jnp.cumsum(uf, axis=1)
    count_base = jnp.arange(1, S + 1, dtype=jnp.float32)
    pooled = []
    for g, w in enumerate(POOL_WINDOWS):
        c = cs[:, :, g]
        prev = jnp.pad(c, ((0, 0), (w, 0), (0, 0)))[:, :S]
        mean = (c - prev) / jnp.minimum(count_base, float(w))[None, :, None]
        pooled.append(mean - uf[:, :, g])
    pooled = jnp.stack(pooled, axis=2).astype(u.dtype)
    mixed = jnp.einsum('bsgc,gcd->bsgd', pooled, w_grp).reshape(B, S, D_INNER) * scale
    return (mixed * jax.nn.silu(z)) @ w_out

def causal_depthwise_conv(x, w):
    return lax.conv_general_dilated(
        x, w[:, None, :].astype(x.dtype), window_strides=(1,),
        padding=[(CONV_WIDTH - 1, 0)], dimension_numbers=('NWC', 'WIO', 'NWC'),
        feature_group_count=x.shape[-1])

def conv_mixer(xn, w_in, conv_w, w_out):
    b, c, h, z = jnp.split(xn @ w_in, 4, axis=-1)
    y = b * causal_depthwise_conv(c * h, conv_w)
    return (y * jax.nn.silu(z)) @ w_out

def apply_rope_2(x, cos, sin):
    half = x.shape[-1] // 2
    x1, x2 = x[..., :half], x[..., half:]
    return jnp.concatenate([x1 * cos - x2 * sin, x2 * cos + x1 * sin], axis=-1).astype(x.dtype)

def causal_block_attention(q_nope, q_rope, k_nope, k_rope, v):
    B, S, H, _ = q_nope.shape
    nb = S // Q_BLOCK
    qn = q_nope.reshape(B, nb, Q_BLOCK, H, QK_NOPE_DIM).transpose(1, 0, 2, 3, 4)
    qr = q_rope.reshape(B, nb, Q_BLOCK, H, QK_ROPE_DIM).transpose(1, 0, 2, 3, 4)
    starts = jnp.arange(nb, dtype=jnp.int32) * Q_BLOCK
    key_idx = jnp.arange(S, dtype=jnp.int32)

    def one_block(args):
        qn_b, qr_b, start = args
        s = (jnp.einsum('bqhd,bkhd->bhqk', qn_b, k_nope).astype(jnp.float32)
             + jnp.einsum('bqhr,bkr->bhqk', qr_b, k_rope).astype(jnp.float32)) * ATTN_SCALE
        q_idx = start + jnp.arange(Q_BLOCK, dtype=jnp.int32)
        mask = key_idx[None, :] <= q_idx[:, None]
        s = jnp.where(mask[None, None], s, jnp.float32(-1e30))
        p = jax.nn.softmax(s, axis=-1).astype(v.dtype)
        return jnp.einsum('bhqk,bkhd->bqhd', p, v)

    o = lax.map(one_block, (qn, qr, starts))
    return o.transpose(1, 0, 2, 3, 4).reshape(B, S, H, V_HEAD_DIM)

def mla_mixer(xn, cos, sin, w_in, q_norm, w_q_up, kv_norm, w_kv_up, w_out):
    B, S, _ = xn.shape
    h = xn @ w_in
    q_lat, kv_lat, k_rope, z = jnp.split(
        h, [Q_LORA_RANK, Q_LORA_RANK + KV_LORA_RANK,
            Q_LORA_RANK + KV_LORA_RANK + QK_ROPE_DIM], axis=-1)
    q = (rms_norm(q_lat, q_norm) @ w_q_up).reshape(B, S, N_HEADS, QK_NOPE_DIM + QK_ROPE_DIM)
    q_nope = q[..., :QK_NOPE_DIM]
    q_rope = apply_rope_2(q[..., QK_NOPE_DIM:], cos[:, :, None, :], sin[:, :, None, :])
    kv = (rms_norm(kv_lat, kv_norm) @ w_kv_up).reshape(B, S, N_HEADS, QK_NOPE_DIM + V_HEAD_DIM)
    k_nope, v = kv[..., :QK_NOPE_DIM], kv[..., QK_NOPE_DIM:]
    k_rope = apply_rope_2(k_rope, cos, sin)
    o = causal_block_attention(q_nope, q_rope, k_nope, k_rope, v)
    return (o.reshape(B, S, D_INNER) * jax.nn.silu(z)) @ w_out

def second_inputs(seed: int = 0) -> dict:
    key = jax.random.key(seed)
    ks = jax.random.split(key, 20)

    def normal(k, shape, scale):
        return jax.random.normal(k, shape, jnp.float32) * scale

    def gain(k, shape):
        return 1.0 + 0.02 * jax.random.normal(k, shape, jnp.float32)

    x = normal(ks[0], (BATCH, SEQ, D_MODEL), 1.0)
    offset = jax.random.randint(ks[1], (BATCH, 1), 0, MAX_POS_OFFSET, dtype=jnp.int32)
    positions = (offset + jnp.arange(SEQ, dtype=jnp.int32)[None, :]).astype(jnp.int32)
    return {
        "x": x,
        "positions": positions,
        "pool_norm": gain(ks[2], (N_POOL, D_MODEL)),
        "pool_w_in": normal(ks[3], (N_POOL, D_MODEL, 2 * D_INNER), D_MODEL ** -0.5),
        "pool_w_grp": normal(ks[4], (N_POOL, N_POOL_GROUPS, POOL_GROUP, POOL_GROUP), POOL_GROUP ** -0.5),
        "pool_scale": gain(ks[5], (N_POOL, D_INNER)),
        "pool_w_out": normal(ks[6], (N_POOL, D_INNER, D_MODEL), D_INNER ** -0.5),
        "conv_norm": gain(ks[7], (N_CONV, D_MODEL)),
        "conv_w_in": normal(ks[8], (N_CONV, D_MODEL, 4 * D_INNER), D_MODEL ** -0.5),
        "conv_w": normal(ks[9], (N_CONV, CONV_WIDTH, D_INNER), CONV_WIDTH ** -0.5),
        "conv_w_out": normal(ks[10], (N_CONV, D_INNER, D_MODEL), D_INNER ** -0.5),
        "mla_norm": gain(ks[11], (N_MLA, D_MODEL)),
        "mla_w_in": normal(ks[12], (N_MLA, D_MODEL, MLA_IN_DIM), D_MODEL ** -0.5),
        "mla_q_norm": gain(ks[13], (N_MLA, Q_LORA_RANK)),
        "mla_w_q_up": normal(ks[14], (N_MLA, Q_LORA_RANK, N_HEADS * (QK_NOPE_DIM + QK_ROPE_DIM)), Q_LORA_RANK ** -0.5),
        "mla_kv_norm": gain(ks[15], (N_MLA, KV_LORA_RANK)),
        "mla_w_kv_up": normal(ks[16], (N_MLA, KV_LORA_RANK, N_HEADS * (QK_NOPE_DIM + V_HEAD_DIM)), KV_LORA_RANK ** -0.5),
        "mla_w_out": normal(ks[17], (N_MLA, D_INNER, D_MODEL), D_INNER ** -0.5),
        "final_norm": gain(ks[18], (D_MODEL,)),
    }

def second_block(x, positions, pool_norm, pool_w_in, pool_w_grp, pool_scale, pool_w_out,
              conv_norm, conv_w_in, conv_w, conv_w_out,
              mla_norm, mla_w_in, mla_q_norm, mla_w_q_up, mla_kv_norm, mla_w_kv_up, mla_w_out,
              final_norm):
    inv_freq = ROPE_BASE ** (-jnp.arange(0, QK_ROPE_DIM, 2, dtype=jnp.float32) / QK_ROPE_DIM)
    angles = positions.astype(jnp.float32)[..., None] * inv_freq
    cos, sin = jnp.cos(angles).astype(x.dtype), jnp.sin(angles).astype(x.dtype)

    for i in range(DEPTH_2):
        kind, j = i % N_MIXERS, i // N_MIXERS
        if kind == 0:
            xn = rms_norm(x, pool_norm[j])
            x = x + pool_mixer(xn, pool_w_in[j], pool_w_grp[j], pool_scale[j], pool_w_out[j])
        elif kind == 1:
            xn = rms_norm(x, conv_norm[j])
            x = x + conv_mixer(xn, conv_w_in[j], conv_w[j], conv_w_out[j])
        else:
            xn = rms_norm(x, mla_norm[j])
            x = x + mla_mixer(xn, cos, sin, mla_w_in[j], mla_q_norm[j], mla_w_q_up[j],
                              mla_kv_norm[j], mla_w_kv_up[j], mla_w_out[j])
    return rms_norm(x, final_norm)


def setup_inputs(seed=0):
    out = dict(first_inputs(seed))
    for name, value in second_inputs(seed + 1).items():
        if name != "x":
            out[name + "_2"] = value
    return out


def reference(
    x, meta_tokens, mix_norm_w, w_in, rec_lb_logits, rec_norm_w, diff_lambda_q1, diff_lambda_k1,
    diff_lambda_q2, diff_lambda_k2, diff_subln_w, w_out, ffn_norm_w, peer_w_query, peer_subkeys,
    peer_u, peer_v, final_norm_w, positions_2, pool_norm_2, pool_w_in_2, pool_w_grp_2,
    pool_scale_2, pool_w_out_2, conv_norm_2, conv_w_in_2, conv_w_2, conv_w_out_2, mla_norm_2,
    mla_w_in_2, mla_q_norm_2, mla_w_q_up_2, mla_kv_norm_2, mla_w_kv_up_2, mla_w_out_2,
    final_norm_2,
):
    x = first_block(
        x, meta_tokens, mix_norm_w, w_in, rec_lb_logits, rec_norm_w, diff_lambda_q1,
        diff_lambda_k1, diff_lambda_q2, diff_lambda_k2, diff_subln_w, w_out, ffn_norm_w,
        peer_w_query, peer_subkeys, peer_u, peer_v, final_norm_w,
    )
    return second_block(
        x, positions_2, pool_norm_2, pool_w_in_2, pool_w_grp_2, pool_scale_2, pool_w_out_2,
        conv_norm_2, conv_w_in_2, conv_w_2, conv_w_out_2, mla_norm_2, mla_w_in_2, mla_q_norm_2,
        mla_w_q_up_2, mla_kv_norm_2, mla_w_kv_up_2, mla_w_out_2, final_norm_2,
    )


_drawn_inputs = setup_inputs


def setup_inputs(seed=0):
    import zlib

    import numpy as np

    out = dict(_drawn_inputs(seed))
    spreads = {}
    factors = {'diff_lambda_k2': 4.173,
     'pool_norm_2': 2.777,
     'pool_scale_2': 3.941,
     'conv_norm_2': 2.79,
     'mla_norm_2': 8.0,
     'mla_q_norm_2': 8.0,
     'mla_kv_norm_2': 8.0,
     'final_norm_2': 2.795}
    for name, (base, spread) in spreads.items():
        noise = np.random.default_rng([zlib.crc32(name.encode()), seed]).standard_normal(out[name].shape)
        drawn = base * np.exp(spread * noise) if base else spread * noise
        out[name] = __import__('jax').numpy.asarray(drawn.astype(out[name].dtype))
    for name, factor in factors.items():
        out[name] = (out[name] * factor).astype(out[name].dtype)
    return out
```

```python
import math
from contextlib import ExitStack

import numpy as np

import concourse.bass as bass
from concourse import mybir

F32 = mybir.dt.float32
F32R = mybir.dt.float32r
I32 = mybir.dt.int32
U32 = mybir.dt.uint32
ALU = mybir.AluOpType
ACT = mybir.ActivationFunctionType
AX_X = mybir.AxisListType.X

P = 128
D = 1024
KD = D // P
T = 512
TT = T // P
M = 16
TM = T + M
EPS = 1e-6
BIG_NEG = -1e30

HEADS = 4
LAM_INIT = 0.8 - 0.6 * math.exp(-0.3 * 0)
GLA_LEVELS = 7

PEER_HEADS = 8
TOPK = 16
KEYS = 128
SLOTS = PEER_HEADS * TOPK

DI = 2048
KI = DI // P
WINDOWS = (2, 4, 8, 16)
MLA_HEADS = 16
QL, KL = 3, 2
MLA_SCALE = (128 + 64) ** -0.5

COLUMNS = 53200
STAGE = 64
EARLY = 64
RING = 4
SLAB = 8 * P

_FIRST = (("ak", 4), ("aq", 4), ("rf", 4), ("rq", 4), ("rg", 4), ("av", 4), ("ri", 4), ("wo", 8), ("wq", 16), ("sk", 2))
_SECOND = (("pin0", 32), ("pgrp0", 8), ("pout0", 16), ("cin", 64), ("cout", 16),
           ("mz", 16), ("mlat", 6), ("mqr", 3), ("mhead", 16), ("mout", 16),
           ("pin1", 32), ("pgrp1", 8), ("pout1", 16))


def _starts(parts, at):
    out = {}
    for name, n in parts:
        out[name] = at
        at += n
    return out, at


SLAB_AT, N_FIRST = _starts(_FIRST, 0)
U_AT = N_FIRST
UM_AT = U_AT + EARLY
_second_at, _end = _starts(_SECOND, N_FIRST + KEYS)
SLAB_AT.update(_second_at)
N_SECOND = _end - N_FIRST - KEYS

TILE_AT, N_TILES = _starts(
    (("ak", 4), ("aq", 4), ("rf", 4), ("rq", 4), ("rg", 4), ("av", 5), ("ri", 5), ("wo", 8), ("wq", 16), ("sk", 16),
     ("early", EARLY), ("u", KEYS - EARLY), ("pin0", 32), ("pgrp0", 16), ("pout0", 8), ("cin", 64), ("cout", 8),
     ("mz", 16), ("mlat", 6), ("mqr", 8), ("mhead", 64), ("mout", 8),
     ("pin1", 32), ("pgrp1", 16), ("pout1", 8)), 0)

def _freed():
    need = {}
    for name, n in _FIRST + _SECOND:
        s0, t0 = SLAB_AT[name], TILE_AT[name]
        for i in range(n):
            if name in ("av", "ri"):
                t = 4
            elif name == "sk":
                t = 15
            elif name.startswith(("wo", "wq")) or name in ("ak", "aq", "rf", "rq", "rg", "cin", "mz", "mlat") or name.startswith("pin"):
                t = i
            elif name in ("cout", "mout") or name.startswith("pout"):
                t = i // 2
            elif name.startswith("pgrp"):
                t = 2 * i + 1
            elif name == "mqr":
                t = (8 * i + 7) // 3
            elif name == "mhead":
                t = 2 if i == 0 else 4 * i + 1
            need[s0 + i] = t0 + t + 1
    for i in range(KEYS):
        need[U_AT + i] = TILE_AT["early"] + i + 1
    return need


FREED = _freed()

NORMS = (("mix", 8),) + tuple((f"att{h}", 1) for h in range(HEADS)) + tuple((f"rec{h}", 1) for h in range(HEADS)) + (
    ("ffn", 8), ("fin1", 8), ("pool0", 8), ("conv", 8), ("mla", 8), ("qlat", 3), ("kvlat", 2), ("pool1", 8), ("fin2", 8))
NORM_I = {name: i for i, (name, _) in enumerate(NORMS)}
NORM_K = dict(NORMS)
NORM_AT, _ = _starts(NORMS, 0)
SPLIT_AT, _ = _starts([(name, n) for name, n in NORMS if name in ("mix", "ffn", "pool0", "conv", "mla", "qlat", "kvlat", "pool1")], 0)

PAR_AT, N_PAR = _starts(
    (("mix", 8), ("ffn", 8), ("fin1", 8), ("pool0", 8), ("pool1", 8), ("conv", 8), ("mla", 8), ("fin2", 8),
     ("qlat", 3), ("kvlat", 2), ("pscale0", 16), ("pscale1", 16), ("convw", 48), ("lb0", 4), ("lb1", 4),
     ("rec", 4), ("att", 1), ("lam", 256)), 0)
CONST_AT, N_CONST = _starts(
    (("ident", P), ("rot", P), ("causal", P), ("iota", P), ("invfreq", 1), ("sign", 1)), 0)


def at(base, i, step):
    return base if i is None else i * step + base


def product(pe, out, w, x, start, stop):
    pe.matmul(out, w[1], x[0], start=start, stop=False)
    pe.matmul(out, w[0], x[1], start=False, stop=False)
    return pe.matmul(out, w[0], x[0], start=False, stop=stop)


class Steps:

    def __init__(self, eng, sem):
        self.eng, self.sem, self.n, self.i, self.per = eng, sem, 0, None, 0

    def __call__(self, ins):
        ins.then_inc(self.sem, 1)
        self.n += 1
        return self.n

    def wait(self, n=None):
        self.eng.wait_ge(self.sem, at(self.n if n is None else n, self.i, self.per))

    def enter(self, i, per):
        self.i, self.per, self.start = i, per, self.n

    def leave(self, turns):
        assert self.n - self.start == self.per, (self.n - self.start, self.per)
        self.n = self.start + self.per * turns
        self.i = None




def build(nc, a):
    with ExitStack() as ctx:
        psA = ctx.enter_context(nc.psum_tensor("ring_banks", [P, 4, 512], F32))
        psB = ctx.enter_context(nc.psum_tensor("work_banks", [P, 4, 512], F32))
        psBf = psB[:, :, :].rearrange("p b n -> p (b n)")
        top = [0]

        base = (nc.sbuf_base + 31) // 32 * 32
        place = {}

        def region(name, *shape, dtype=F32):
            place[name] = top[0]
            top[0] += (int(np.prod(shape)) + 7) // 8 * 8
            assert top[0] <= COLUMNS, (name, top[0])
            return nc.alloc_sbuf_tensor_at(name, [P, *shape], dtype, offset=base + 4 * place[name])[:]

        def rounded(name, over, *shape):
            return nc.alloc_sbuf_tensor_at(name, [P, *shape], F32R, offset=base + 4 * place[over])[:]

        def sem(name):
            return ctx.enter_context(nc.semaphore(name))

        hT = region("hT", KD, T)
        xn = region("xn", KD, TM)
        spare = region("spare", KD * TM)
        xx = rounded("xx", "xn", 2 * KD, TM)
        xlo, xh = xx[:, 0:KD, :], xx[:, KD:2 * KD, :]
        slot = [region(f"slot{r}", 8, P) for r in range(RING)]
        wlo = [rounded(f"wlo{r}", f"slot{r}", 8, P) for r in range(RING)]
        whi = [region(f"whi{r}", 8, P, dtype=F32R) for r in range(RING)]
        sq = region("sq", 2, TM)
        ms = region("ms", TM)
        rt = region("rt", TM)
        rstd = region("rstd", TM)
        newt = region("newt", TM)
        ones = region("ones", P)
        const = region("const", N_CONST)
        par = region("par", N_PAR)
        ident = const[:, 0:P]
        rot = const[:, CONST_AT["rot"]:CONST_AT["rot"] + P]
        causal = const[:, CONST_AT["causal"]:CONST_AT["causal"] + P]
        iota = const[:, CONST_AT["iota"]:CONST_AT["iota"] + P]

        def pcol(name, i=0, n=1):
            c = PAR_AT[name] + i
            return par[:, c:c + n]

        stay = top[0]

        hM = region("hM", KD, M)
        kk = region("kk", HEADS, TM)
        cum = region("cum", HEADS, TM)
        q_rec = region("q_rec", HEADS, T)
        gate = region("gate", HEADS, T)
        ri = region("ri", TT + 1, T)
        raw = region("raw", HEADS * (TM + T))
        kraw = raw[:, 0:HEADS * TM].rearrange("p (h t) -> p h t", h=HEADS)
        qraw = raw[:, HEADS * TM:].rearrange("p (h t) -> p h t", h=HEADS)
        mixed = raw[:, 0:KD * T].rearrange("p (k t) -> p k t", k=KD)
        mixed_lo = rounded("mixed_lo", "raw", KD, T)
        reset = spare[:, 0:HEADS * TM]
        lgm = spare[:, HEADS * TM:HEADS * TM + (GLA_LEVELS + 1) * P].rearrange("p (l t) -> p l t", t=P)
        lb = region("lb", 4, 4)
        el = region("el", HEADS, TT + 1)
        lamc = region("lamc", 8)
        lamp = region("lamp", 2, 64)
        shared = top[0]
        kT = region("kT", HEADS, TM)
        qT = region("qT", HEADS, T)
        ropt = region("ropt", TM)
        cosA = region("cosA", TM)
        sinA = region("sinA", TM)
        av = region("av", TT + 1, T)
        probs = region("probs", 2, TM)
        wgt = region("wgt", TM)
        wT = region("wT", TT + 1, P)
        smax = region("smax", 2)
        nmax = region("nmax", 2)
        ssum = region("ssum", 2)
        rsum = region("rsum", 2)
        top[0] = shared
        kd = region("kd", HEADS, TM)
        qd = region("qd", HEADS, T)
        lev = [region(f"lev{x}", HEADS, T) for x in range(2)]
        state = region("state", TT, HEADS, P)
        kdT = region("kdT", HEADS, TT + 1, P)
        pairT = xn[:, 0:4, 0:T]

        top[0] = stay
        it_, jt_, gt_ = region("slot_row", T), region("slot_column", T), region("slot_gate", T)
        early = [region(f"early{b}", T) for b in range(4)]
        peer = top[0]
        stage = [region(f"stage{b}", KEYS // 4, 4, STAGE) for b in range(2)]
        ones_at = top[0]
        oneI = region("oneI", 16, P)
        oneJ = region("oneJ", 16, P)
        vbuf = [region("v0", 4, D)]
        top[0] = ones_at
        vhi = [region("vhi0", 4, D, dtype=F32R)]
        top[0] = peer
        qp = region("qp", 16, T)
        sc = [region(f"scores{tt}", 16, P) for tt in range(TT)]
        sc2 = region("sc2", 2, P)
        sv = region("sv", 16, TOPK)
        si = region("si", 16, TOPK)
        sif = region("sif", 16, TOPK)
        cand = region("cand", PEER_HEADS, 256)
        cand2 = region("cand2", 2, 256)
        tops = region("tops", PEER_HEADS, TOPK)
        posu = region("posu", PEER_HEADS, TOPK)
        abu = region("abu", 2, SLOTS)
        abf = region("abf", 2, SLOTS)
        hot = region("hot", SLOTS, TOPK)
        sel = region("sel", 2, SLOTS)
        gates = region("gates", PEER_HEADS, TOPK)
        gsum = region("gsum", PEER_HEADS)
        top[0] = stay
        vbuf.append(region("v1", 4, D))
        vhi.append(region("vhi1", 4, D, dtype=F32R))
        vlo = [rounded(f"vlo{b}", f"v{b}", 4, D) for b in range(2)]
        gbuf = region("gbuf", 2, T // STAGE, 4, STAGE)
        ghi = rounded("ghi", "gbuf", 2, T // STAGE, 4, STAGE)
        ge = region("ge", 2, 4, T)
        glo = rounded("glo", "ge", 2, 4, T)

        top[0] = stay
        pooled = region("pooled_lo", KI, T, dtype=F32R)
        pooledh = region("pooled_hi", KI, T, dtype=F32R)
        zb = region("zb", KI, T)
        zb_lo = rounded("zb_lo", "zb", KI, T)
        upad = region("upad", 2, TM)
        win = [region(f"window{x}", TM) for x in range(2)]
        rcnt = region("rcnt", 4, M)
        pfew = region("pfew", M)
        ptmp = region("ptmp", T)
        top[0] = stay
        yb = region("y_lo", KI, T, dtype=F32R)
        yh = region("y_hi", KI, T, dtype=F32R)
        cbuf = region("cbuf", 4, T)
        chpad = region("chpad", T + 2)
        cacc = region("cacc", 2, T)
        top[0] = stay
        mz = region("mz", KI, T)
        mz_lo = rounded("mz_lo", "mz", KI, T)
        lat = region("lat", QL + KL + 1, T)
        lat_hi = rounded("lat_hi", "lat", QL + KL, T)
        latn = region("latn", QL + KL, T)
        lat_lo = rounded("lat_lo", "latn", QL + KL, T)
        ropek = region("ropek", T)
        cos2 = region("cos2", T)
        sin2 = region("sin2", T)
        rn = region("rn", T)
        qrope = region("qrope", 8, T)
        qh = region("qh", 2, T)
        qrh = region("qrh", 2, T)
        kh = region("kh", 2, T)
        vh = region("vh", 2, TT, P)
        mp = region("mp", 2, T)
        posi, ang = mp[:, 0, :], mp[:, 1, :]
        mpT = region("mpT", 2, TT, P)
        obuf = region("obuf", 2, T)
        mmax = region("mmax", 2)
        mneg = region("mneg", 2)
        msum = region("msum", 2)
        mrec = region("mrec", 2)

        s_in = sem("inputs_loaded")
        s_tab = sem("tables_loaded")
        s_tab2 = sem("second_tables_loaded")
        s_tab3 = sem("gla_tables_loaded")
        s_ones = sem("ones_set")
        split = sem("slab_split")
        xsc = sem("normed_scaled")
        xhi = sem("normed_hi_ready")
        m_h = sem("mixed_split")
        z_h = sem("gated_split")
        p_vs = sem("v_split")
        loaded = [sem(f"slab{r}_loaded") for r in range(RING)]
        done = sem("tile_computed")
        out_ = sem("tile_taken")
        sqr = sem("square_ready")
        squ = sem("square_summed")
        msr = sem("mean_square_ready")
        rtr = sem("root_ready")
        xnr = sem("normed_ready")
        own = sem("vector_steps")
        pool_own = sem("gpsimd_steps")
        s_lam = sem("lambda_sums")
        s_lame = sem("lambda_exps")
        s_perm = sem("rotated")
        s_rope = sem("roped")
        s_cst = sem("first_rope_ready")
        s_f = sem("f_ready")
        s_g = sem("log_f_ready")
        a_s = sem("att_scores")
        a_m = sem("att_max")
        a_p = sem("att_probs")
        a_w = sem("att_weights")
        a_t = sem("att_weights_transposed")
        a_c = sem("att_weights_copied")
        a_o = sem("att_out")
        a_oc = sem("att_out_copied")
        n_m = sem("mixed_ready")
        g_d = sem("gla_difference")
        g_e = sem("gla_exp")
        g_l = sem("gla_level_ready")
        g_a = sem("gla_pairs")
        g_c = sem("gla_pairs_copied")
        g_t = sem("gla_k_transposed")
        g_k = sem("gla_k_copied")
        g_u = sem("gla_update")
        g_s = sem("gla_state")
        g_q = sem("gla_q_ready")
        g_o = sem("gla_out")
        g_oc = sem("gla_out_copied")
        wo_d = sem("residual_added")
        p_x = sem("topk_of_tile")
        p_tp = sem("slots_transposed")
        p_tc = sem("slots_copied")
        p_ge = sem("gate_difference")
        p_gx = sem("gate_exp")
        p_oh = sem("onehots_ready")
        p_om = sem("onehots_multiplied")
        p_st = sem("gates_staged")
        p_gw = [sem(f"gates_written{b}") for b in range(2)]
        p_hw = [sem(f"early_written{b}") for b in range(4)]
        p_hl = [sem(f"early_loaded{b}") for b in range(2)]
        p_v = [sem(f"v_loaded{b}") for b in range(2)]
        p_g = [sem(f"gates_loaded{b}") for b in range(2)]
        p_w = sem("expert_weights_ready")
        p_y = sem("expert_out")
        p_ya = sem("expert_out_added")
        u_p = sem("pooled_ready")
        u_f = sem("pooled_first_tokens")
        u_a = sem("pool_activated")
        c_y = sem("conv_ready")
        m_tab = sem("second_rope_ready")
        m_ang = sem("angles_ready")
        m_s = sem("mla_scores")
        m_m = sem("mla_max")
        m_p = sem("mla_probs")
        m_w = sem("mla_probs_scaled")
        m_t = sem("mla_transposed")
        m_c = sem("mla_probs_copied")
        m_v = sem("mla_values_summed")
        m_y = sem("mla_gated")
        s_out = sem("output_written")

        block = ctx.enter_context(nc.Block())

        def slab(s):
            return whi[s % RING], wlo[s % RING]

        def pick(parts, *index):
            return tuple(p[(slice(None),) + index] for p in parts)

        def slab_in(eng, s, i=None, per=RING):
            eng.wait_ge(split, at(s + 1 - 2 * (s > SLAB_AT["sk"]), i, per))

        @block.sync
        def _(sp):
            def load_slab(src, s, j, i=None):
                if s >= RING:
                    step = 0 if i is None else FREED[s] - FREED[s - RING]
                    sp.wait_ge(done, at(FREED[s - RING], i, step))
                piece = src[j] if i is None else src[bass.ds(i * RING + j, 1)].rearrange("o p n -> p (o n)")
                sp.dma_start(slot[s % RING], piece.rearrange("p (k m) -> p k m", k=8)).then_inc(loaded[s % RING], 16)

            def layer(name, n):
                s0 = SLAB_AT[name]
                src, base = (a["w1"], 0) if s0 < N_FIRST else (a["w2"], N_FIRST + KEYS)
                turns = (n - RING) // RING - (name == "mhead")
                for s in range(s0, s0 + min(n, RING)):
                    load_slab(src, s, s - base)
                if n <= RING:
                    return
                s = s0 + RING
                if name == "mhead":
                    for s in range(s0 + RING, s0 + 2 * RING):
                        load_slab(src, s, s - base)
                    s = s0 + 2 * RING
                if turns > 1:
                    with sp.Fori(0, turns) as i:
                        for r in range(RING):
                            load_slab(src, s + r, s + r - base, i)
                    s += turns * RING
                for s in range(s, s0 + n):
                    load_slab(src, s, s - base)

            sp.dma_start(hT, a["xT"]).then_inc(s_in, 16)
            sp.dma_start(hM, a["metaT"]).then_inc(s_in, 16)
            sp.dma_start(const, a["const"]).then_inc(s_in, 16)
            sp.dma_start(par, a["par"]).then_inc(s_in, 16)
            layer("ak", 4)
            sp.dma_start(cosA, a["cosA"]).then_inc(s_tab, 16)
            sp.dma_start(sinA, a["sinA"]).then_inc(s_tab, 16)
            for name, n in _FIRST[1:]:
                if name == "wo":
                    sp.wait_ge(done, TILE_AT["ri"] + TT + 1)
                    sp.dma_start(lgm, a["levels"]).then_inc(s_tab3, 16)
                    sp.dma_start(reset, a["reset"]).then_inc(s_tab3, 16)
                layer(name, n)

            for s in range(U_AT, U_AT + RING):
                load_slab(a["u"], s, s - U_AT)
            def next_u(u, i=None):
                s = U_AT + RING + u
                sp.wait_ge(done, at(FREED[s - RING], i, 4))
                piece = a["u"][s - U_AT] if i is None else a["u"][bass.ds(i * 4 + (s - U_AT), 1)].rearrange("o p n -> (o p) n")
                sp.dma_start(slot[s % RING], piece.rearrange("p (k m) -> p k m", k=8)).then_inc(loaded[s % RING], 16)
                sp.wait_ge(out_, at(TILE_AT["early"] + u + 1, i, 4))
                dst = a["early"][u] if i is None else a["early"][bass.ds(i * 4 + u, 1)].rearrange("o p t -> (o p) t")
                sp.dma_start(dst, early[u % 4]).then_inc(p_hw[u % 4], 16)

            with sp.Fori(0, EARLY // 2 // 4) as i:
                for r in range(4):
                    next_u(r, i)
            for t in range(T // STAGE):
                for r in range(4):
                    next_u(EARLY // 2 + 4 * t + r)
                if t == 1:
                    sp.wait_ge(p_tc, TT)
                    sp.dma_start(vbuf[0], a["v"][0].rearrange("p (j d) -> p j d", j=4)).then_inc(p_v[0], 16)
                sp.wait_ge(p_st, STAGE // 4 * (t + 1))
                for c in range(2):
                    sp.dma_start(a["gates"][16 * c:16 * c + 16, :, t].rearrange("g i n -> i g n"),
                                 stage[t % 2][:, 16 * c:16 * c + 16].rearrange("p g r t -> p g (r t)")).then_inc(p_gw[t % 2], 16)
            for b in range(2):
                sp.wait_ge(p_gw[b], T // STAGE // 2 * 2 * 16)
            for b in range(4):
                sp.wait_ge(p_hw[b], EARLY // 4 * 16)

            def group(g, b, gi):
                vsrc = a["v"][g] if gi is None else a["v"][bass.ds(gi * 2 + g, 1)].rearrange("o p n -> (o p) n")
                gsrc = a["gates"][g] if gi is None else a["gates"][bass.ds(gi * 2 + g, 1)].rearrange("o i t n -> (o i) t n")
                if gi is not None:
                    sp.wait_ge(p_y, gi * 16 + 8 * (g - 1))
                sp.dma_start(gbuf[:, b].rearrange("p t r n -> p t (r n)"), gsrc).then_inc(p_g[b], 16)
                esrc = a["early"][2 * g:2 * g + 2] if gi is None else a["early"][bass.ds(gi * 4 + 2 * g, 2)]
                sp.dma_start(ge[:, b, 0:2, :], esrc.rearrange("r p t -> p r t")).then_inc(p_hl[b], 16)
                if g:
                    sp.dma_start(vbuf[b], vsrc.rearrange("p (j d) -> p j d", j=4)).then_inc(p_v[b], 16)

            group(0, 0, None)
            group(1, 1, None)
            with sp.Fori(0, 15) as i:
                for b in range(2):
                    for x in range(2):
                        s = UM_AT + 2 * (2 + b) + x
                        sp.wait_ge(done, at(FREED[s - RING], i, 4))
                        sp.dma_start(slot[s % RING], a["u"][bass.ds(i * 4 + (s - U_AT), 1)]
                                     .rearrange("o p (k m) -> p (o k) m", k=8)).then_inc(loaded[s % RING], 16)
                    group(2 + b, b, i)
            sp.wait_ge(xnr, NORM_AT["pool0"])
            sp.dma_start(rcnt, a["counts"]).then_inc(s_tab2, 16)
            for name, n in _SECOND:
                layer(name, n)
                if name == "cout":
                    sp.wait_ge(done, TILE_AT["cout"] + 8)
                    sp.dma_start(posi.bitcast(I32), a["positions"]).then_inc(s_tab2, 16)
                if name == "mout":
                    sp.wait_ge(done, TILE_AT["mout"] + 8)
                    sp.dma_start(rcnt, a["counts"]).then_inc(s_tab2, 16)
            sp.wait_ge(xnr, NORM_AT["fin2"] + KD)
            sp.dma_start(a["out"], xn[:, :, 0:T]).then_inc(s_out, 16)
            sp.wait_ge(s_out, 16)

        @block.gpsimd
        def _(pool):
            pool.memset(ones, 1.0).then_inc(s_ones, 1)
            one = ones.unsqueeze(1).to_broadcast([P, 8, P])
            halves_ = Steps(pool, pool_own)
            pool.wait_ge(s_ones, 1)

            def split_slab(s, i=None):
                pool.wait_ge(loaded[s % RING], at(16 * (s // RING + 1), i, 16))
                (w_hi, w_lo), w = slab(s), slot[s % RING]
                halves_(pool.tensor_tensor(w_hi, w, one, ALU.mult))
                halves_.wait()
                pool.tensor_tensor(w_lo, w, w_hi.bitcast(F32), ALU.subtract).then_inc(split, 1)

            def split_slabs(s0, n):
                with pool.Fori(0, n // RING) as i:
                    halves_.enter(i, RING)
                    for r in range(RING):
                        split_slab(s0 + r, i)
                    halves_.leave(n // RING)
                for s in range(s0 + n // RING * RING, s0 + n):
                    split_slab(s)

            def split_v(g, b, gi):
                pool.wait_ge(p_v[b], at(16 * (g // 2 + 1), gi, 16))
                for r in range(4):
                    v_hi, v = (x[b][:, r, :].rearrange("p (k m) -> p k m", k=8) for x in (vhi, vbuf))
                    halves_(pool.tensor_tensor(v_hi, v, one, ALU.mult))
                halves_.wait()
                for r in range(4):
                    ins = pool.tensor_tensor(vlo[b][:, r, :], vbuf[b][:, r, :], vhi[b][:, r, :].bitcast(F32), ALU.subtract)
                ins.then_inc(p_vs, 1)

                return
                return
            split_slabs(0, SLAB_AT["sk"])
            split_slabs(U_AT, EARLY + 4)
            pool.wait_ge(p_om, T // 4)
            split_v(0, 0, None)
            with pool.Fori(0, 15) as i:
                halves_.enter(i, 12)
                for b in range(2):
                    for x in range(2):
                        s = UM_AT + 2 * (2 + b) + x
                        pool.wait_ge(loaded[s % RING], at(16 * (s // RING + 1), i, 16))
                        (w_hi, w_lo), w = slab(s), slot[s % RING]
                        halves_(pool.tensor_tensor(w_hi, w, one, ALU.mult))
                        halves_.wait()
                        pool.tensor_tensor(w_lo, w, w_hi.bitcast(F32), ALU.subtract).then_inc(split, 1)
                    split_v(1 + b, 1 - b, i)
                halves_.leave(15)
            split_v(31, 1, None)
            split_slabs(U_AT + KEYS, N_SECOND)

        @block.tensor
        def _(pe):
            def norm(name, meta=False):
                n, k0, kn = NORM_I[name], NORM_AT[name], NORM_K[name]
                if n:
                    pe.wait_ge(msr, n)
                for k in range(kn):
                    pe.wait_ge(sqr, k0 + k + 1)
                    if meta:
                        pe.matmul(psB[:, 2, 0:M], ones, sq[:, (k0 + k) % 2, T:TM], start=(k == 0), stop=(k == kn - 1))
                    pe.matmul(psB[:, 3, :], ones, sq[:, (k0 + k) % 2, 0:T],
                              start=(k == 0), stop=(k == kn - 1)).then_inc(squ, 1)

            def free_bank(t, i=None, per=0):
                if t >= RING:
                    pe.wait_ge(out_, at(t - RING + 1, i, per))
                return psA[:, t % RING, :]

            def project8(name, n, x=(xh, xlo), meta=False):
                s0, t0 = SLAB_AT[name], TILE_AT[name]

                def turn(i):
                    for r in range(4):
                        slab_in(pe, s0 + r, i)
                        bank = free_bank(t0 + r, i, 4)
                        w = slab(s0 + r)
                        if meta:
                            for k in range(8):
                                product(pe, psB[:, r, 0:M], pick(w, k), pick(x, k, slice(T, TM)), k == 0, k == 7)
                        for k in range(8):
                            mm = product(pe, bank, pick(w, k), pick(x, k, slice(0, T)), k == 0, k == 7)
                        mm.then_inc(done, 1)

                if n == 4:
                    turn(None)
                else:
                    with pe.Fori(0, n // 4) as i:
                        turn(i)

            def project16(name, x):
                s0, t0 = SLAB_AT[name], TILE_AT[name]
                with pe.Fori(0, 2) as i:
                    for r in range(4):
                        bank = free_bank(t0 + r, i, 4)
                        for half in range(2):
                            slab_in(pe, s0 + 2 * r + half, i, 8)
                            for k in range(8):
                                mm = product(pe, bank, pick(slab(s0 + 2 * r + half), k),
                                             pick(x, 8 * half + k, slice(0, T)), half + k == 0, half * 8 + k == 15)
                        mm.then_inc(done, 1)

            def tokens_first(name):
                s0, t0 = SLAB_AT[name], TILE_AT[name]
                for r in range(4):
                    slab_in(pe, s0 + r)
                for t in range(TT + 1):
                    bank = free_bank(t0 + t)
                    rows = P if t < TT else M
                    for k in range(8):
                        w = tuple(v.rearrange("p k m -> p (k m)")[:, k % 2 * 512:k % 2 * 512 + 512] for v in slab(s0 + k // 2))
                        mm = product(pe, bank[0:rows, :], pick((xh, xlo), k, slice(t * P, t * P + rows)), w, k == 0, k == 7)
                    mm.then_inc(done, 1)

            pe.wait_ge(s_ones, 1)
            pe.wait_ge(s_in, 64)
            norm("mix", meta=True)
            pe.wait_ge(xnr, KD)
            project8("ak", 4, meta=True)
            project8("aq", 4)
            project8("rf", 4, meta=True)
            project8("rq", 4)
            project8("rg", 4)
            for j in range(2 * HEADS):
                pe.wait_ge(out_, j + 1)
                if j >= 2:
                    pe.wait_ge(s_rope, j - 1)
                src = kraw[:, j, :] if j < HEADS else qraw[:, j - HEADS, :]
                if j < HEADS:
                    pe.matmul(psB[:, 2 + j % 2, 0:M], rot, src[:, T:TM], start=True, stop=True)
                pe.matmul(psB[:, j % 2, :], rot, src[:, 0:T], start=True, stop=True).then_inc(s_perm, 1)
            tokens_first("av")
            tokens_first("ri")

            pe.wait_ge(s_rope, 2 * HEADS)
            pe.wait_ge(out_, TILE_AT["av"] + 5)

            def scores(n):
                h, i = divmod(n, TT)
                lo = T - (i + 1) * P
                if n:
                    pe.wait_ge(a_p, n)
                for p in range(2):
                    q = qT[64 * p:64 * p + 64, h, i * P:(i + 1) * P]
                    pe.matmul(psBf[:, 1024 * p + lo:1024 * p + T], q, kT[64 * p:64 * p + 64, h, 0:T - lo],
                              start=True, stop=False)
                    pe.matmul(psBf[:, 1024 * p + T - P:1024 * p + T], ident, causal, start=False, stop=True)
                    mm = pe.matmul(psBf[:, 1024 * p + T:1024 * p + TM], q, kT[64 * p:64 * p + 64, h, T:TM],
                                   start=True, stop=True)
                mm.then_inc(a_s, 1)

            def weigh(n):
                h, i = divmod(n, TT)
                lo = T - (i + 1) * P
                pe.wait_ge(a_w, n + 1)
                if n == 0:
                    pe.wait_ge(out_, TILE_AT["ri"] + 5)
                else:
                    pe.wait_ge(a_c, n)
                for kb in range(i + 1):
                    pe.transpose(psA[:, 0, kb * P:(kb + 1) * P], wgt[:, lo + kb * P:lo + (kb + 1) * P], ident)
                pe.transpose(psA[0:M, 1, 0:P], wgt[:, T:TM], ident).then_inc(a_t, 1)
                pe.wait_ge(a_c, n + 1)
                if i == 0 and h >= 2:
                    pe.wait_ge(a_oc, h - 1)
                o = psA[:, 2 + h % 2, i * P:(i + 1) * P]
                for kb in range(i + 1):
                    pe.matmul(o, av[:, kb, h * P:(h + 1) * P], wT[:, kb, :], start=(kb == 0), stop=False)
                pe.matmul(o, av[0:M, TT, h * P:(h + 1) * P], wT[0:M, TT, :], start=False, stop=True).then_inc(a_o, 1)

            scores(0)
            for n in range(HEADS * TT):
                if n + 1 < HEADS * TT:
                    scores(n + 1)
                weigh(n)
            for h in range(HEADS):
                if h == 0:
                    pe.wait_ge(a_p, HEADS * TT)
                norm(f"att{h}")

            pe.wait_ge(a_oc, HEADS)
            for lv in range(GLA_LEVELS + 1):
                if lv < GLA_LEVELS:
                    pe.wait_ge(g_l, lv + 1)
                for h in range(HEADS):
                    if lv:
                        pe.wait_ge(g_c, HEADS * (lv - 1) + h + 1)
                    for c in range(TT):
                        if lv < GLA_LEVELS:
                            left = right = lev[lv % 2][:, h, c * P:(c + 1) * P]
                        else:
                            left, right = kk[:, h, c * P:(c + 1) * P], q_rec[:, h, c * P:(c + 1) * P]
                        mm = pe.matmul(psA[:, h, c * P:(c + 1) * P], left, right, start=True, stop=True)
                    mm.then_inc(g_a, 1)
            for h in range(HEADS):
                if h == 0:
                    pe.wait_ge(g_q, 1)
                    pe.wait_ge(msr, NORM_I["att3"] + 1)
                if h >= 2:
                    pe.wait_ge(g_k, h - 1)
                for c in range(TT):
                    pe.transpose(psB[:, h % 2, c * P:(c + 1) * P], kd[:, h, c * P:(c + 1) * P], ident)
                pe.transpose(psB[0:M, 2 + h % 2, 0:P], kd[:, h, T:TM], ident).then_inc(g_t, 1)
            pe.wait_ge(g_k, HEADS)
            for n in range(TT):
                if n >= 2:
                    pe.wait_ge(g_s, n - 1)
                for h in range(HEADS):
                    if n == 0:
                        left, right = kdT[0:M, h, TT, :], ri[0:M, TT, h * P:(h + 1) * P]
                    else:
                        left, right = kdT[:, h, n - 1, :], ri[:, n - 1, h * P:(h + 1) * P]
                    mm = pe.matmul(psB[:, n % 2, h * P:(h + 1) * P], left, right, start=True, stop=True)
                mm.then_inc(g_u, 1)
            pe.wait_ge(g_c, HEADS * (GLA_LEVELS + 1))
            pe.wait_ge(g_s, TT)
            for h in range(HEADS):
                for c in range(TT):
                    o = psA[:, h, c * P:(c + 1) * P]
                    pe.matmul(o, ri[:, c, h * P:(h + 1) * P], pairT[:, h, c * P:(c + 1) * P], start=True, stop=False)
                    mm = pe.matmul(o, state[:, c, h, :], qd[:, h, c * P:(c + 1) * P], start=False, stop=True)
                mm.then_inc(g_o, 1)
            for h in range(HEADS):
                norm(f"rec{h}")
            pe.wait_ge(n_m, HEADS)
            pe.wait_ge(g_oc, HEADS)
            pe.wait_ge(m_h, KD)
            project8("wo", 8, x=(xh, mixed_lo))
            norm("ffn")

            pe.wait_ge(xnr, NORM_AT["ffn"] + KD)
            project8("wq", 16)
            for s in (SLAB_AT["sk"], SLAB_AT["sk"] + 1):
                pe.wait_ge(loaded[s % RING], 16 * (s // RING + 1))
            pe.wait_ge(out_, TILE_AT["wq"] + 16)
            t0 = TILE_AT["sk"]
            for tt in range(TT):
                for b in range(4):
                    bank = free_bank(t0 + 4 * tt + b)
                    for c in range(4):
                        hp = 4 * b + c
                        w = slot[(SLAB_AT["sk"] + hp // 8) % RING][:, hp % 8, :]
                        mm = pe.matmul(bank[:, c * P:(c + 1) * P], qp[:, hp, tt * P:(tt + 1) * P], w, start=True, stop=True)
                    mm.then_inc(done, 1)
            def hidden_tile(s, t, i):
                slab_in(pe, s, i)
                bank = free_bank(t, i, 4)
                for k in range(8):
                    mm = product(pe, bank, pick(slab(s), k), pick((xh, xlo), k, slice(0, T)), k == 0, k == 7)
                mm.then_inc(done, 1)

            def early_tile(u, i):
                hidden_tile(U_AT + u, TILE_AT["early"] + u, i)

            for tt in range(TT):
                with pe.Fori(0, 2) as i:
                    for r in range(4):
                        early_tile(8 * tt + r, i)
                pe.wait_ge(p_x, tt + 1)
                if tt >= 2:
                    pe.wait_ge(p_tc, tt - 1)
                b = psB[:, tt % 2, :]
                pe.transpose(b[:, 0:P], sel[:, 0, :], ident)
                pe.transpose(b[:, P:2 * P], sel[:, 1, :], ident)
                pe.transpose(b[:, 2 * P:3 * P], gates.rearrange("p h k -> p (h k)"), ident).then_inc(p_tp, 1)

            def spots(n0, i):
                for n in range(n0, n0 + STAGE // 4):
                    q = n % 4
                    pe.wait_ge(p_oh, at(n + 1, i, STAGE // 4))
                    if n >= 4:
                        pe.wait_ge(p_st, at(n - 3, i, STAGE // 4))
                    for u in range(4):
                        mm = pe.matmul(psB[:, q, u * P:(u + 1) * P], oneI[:, 4 * q + u, :],
                                       oneJ[:, 4 * q + u, :], start=True, stop=True)
                    mm.then_inc(p_om, 1)
                    if q == 3:
                        early_tile(EARLY // 2 + n // 4, i)

            pe.wait_ge(p_tc, TT)
            spots(0, None)
            with pe.Fori(0, T // STAGE - 1) as i:
                spots(STAGE // 4, i)

            def hidden(g, b, gi):
                for x in range(2):
                    hidden_tile(UM_AT + 2 * g + x, TILE_AT["u"] + 2 * g + x, gi)

            def spread(g, b, gi):
                pe.wait_ge(p_w, at(4 * g + 4, gi, 8))
                pe.wait_ge(p_vs, at(g + 1, gi, 2))
                for d in range(KD):
                    if g or d >= 4:
                        pe.wait_ge(p_ya, at(8 * g + d - 3, gi, 16))
                    for r in range(4):
                        mm = product(pe, psB[:, d % 4, :], pick((vhi[b], vlo[b]), r, slice(d * P, (d + 1) * P)),
                                     (ghi[:, b, :, r, :], glo[:, b, r, :]), r == 0, r == 3)
                    mm.then_inc(p_y, 1)

            hidden(0, 0, None)
            hidden(1, 1, None)
            pe.wait_ge(p_st, T // 4)
            spread(0, 0, None)
            hidden(2, 0, None)
            spread(1, 1, None)
            with pe.Fori(0, 14) as i:
                hidden(3, 1, i)
                spread(2, 0, i)
                hidden(4, 0, i)
                spread(3, 1, i)
            hidden(31, 1, None)
            spread(30, 0, None)
            spread(31, 1, None)
            pe.wait_ge(p_ya, 8 * 32)
            norm("fin1")

            def pool_layer(j):
                norm(f"pool{j}")
                pe.wait_ge(xnr, NORM_AT[f"pool{j}"] + KD)
                project8(f"pin{j}", 32)
                pe.wait_ge(u_p, 16 * (j + 1))
                name = f"pgrp{j}"
                s0, t0 = SLAB_AT[name], TILE_AT[name]
                with pe.Fori(0, 2) as i:
                    for r in range(4):
                        slab_in(pe, s0 + r, i)
                        for half in range(2):
                            t = 2 * r + half
                            bank = free_bank(t0 + t, i, 8)
                            for k in range(4):
                                x = tuple(v[:, bass.ds(i * 8 + (t // 4 * 4 + k), 1), :].rearrange("p o n -> p (o n)")
                                          for v in (pooledh, pooled))
                                mm = product(pe, bank, pick(slab(s0 + r), 4 * half + k), x, k == 0, k == 3)
                            mm.then_inc(done, 1)
                pe.wait_ge(z_h, 16 * (j + 1))
                project16(f"pout{j}", (xx, zb_lo))

            pool_layer(0)
            norm("conv")
            pe.wait_ge(xnr, NORM_AT["conv"] + KD)
            project8("cin", 64)
            pe.wait_ge(c_y, 16)
            project16("cout", (yh, yb))

            norm("mla")
            pe.wait_ge(xnr, NORM_AT["mla"] + KD)
            project8("mz", 16)
            for r in range(6):
                s, t = SLAB_AT["mlat"] + r, TILE_AT["mlat"] + r
                slab_in(pe, s)
                bank = free_bank(t)
                for k in range(8):
                    mm = product(pe, bank, pick(slab(s), k), pick((xh, xlo), k, slice(0, T)), k == 0, k == 7)
                mm.then_inc(done, 1)
            norm("qlat")
            norm("kvlat")
            pe.wait_ge(out_, TILE_AT["mlat"] + 6)
            pe.matmul(psB[:, 0, :], rot, lat[:, QL + KL, :], start=True, stop=True).then_inc(s_perm, 1)
            pe.wait_ge(xnr, NORM_AT["kvlat"] + KL)
            s0, t0 = SLAB_AT["mqr"], TILE_AT["mqr"]
            for t in range(8):
                bank = free_bank(t0 + t)
                for k in range(QL):
                    w = 3 * t + k
                    if w % 8 == 0:
                        slab_in(pe, s0 + w // 8)
                    mm = product(pe, bank, pick(slab(s0 + w // 8), w % 8), pick((lat_hi, lat_lo), k), k == 0, k == QL - 1)
                mm.then_inc(done, 1)
            for t in range(8):
                pe.wait_ge(out_, t0 + t + 1)
                pe.wait_ge(s_rope, 2 * HEADS + max(t, 1))
                pe.matmul(psB[:, (t + 1) % 2, :], rot, qrope[:, t, :], start=True, stop=True).then_inc(s_perm, 1)
            pe.wait_ge(s_rope, 2 * HEADS + 9)

            def head_tile(x, h, i):
                s = SLAB_AT["mhead"] + h
                t = TILE_AT["mhead"] + (x if h == 0 else 4 * h - 1 + x)
                w, ln = slab(s), (lat_hi, lat_lo)
                bank = free_bank(t, i, 16)
                if x == 0:
                    slab_in(pe, s, i)
                    for k in range(QL):
                        mm = product(pe, bank, pick(w, k), pick(ln, k), k == 0, k == QL - 1)
                elif x == 1:
                    for k in range(KL):
                        mm = product(pe, bank, pick(w, QL + k), pick(ln, QL + k), k == 0, k == KL - 1)
                else:
                    for tt in range(TT):
                        for k in range(KL):
                            mm = product(pe, bank[:, tt * P:(tt + 1) * P], pick(ln, QL + k, slice(tt * P, (tt + 1) * P)),
                                         pick(w, QL + KL + k), k == 0, k == KL - 1)
                mm.then_inc(done, 1)

            def mla_scores(c, i):
                h, n = divmod(c, TT)
                e, keys = h % 2, (n + 1) * P
                if n == 0:
                    pe.wait_ge(out_, at(TILE_AT["mhead"] + (2 if h == 0 else 4 * h + 1), i, 16))
                if c >= 2:
                    pe.wait_ge(m_p, at(c - 1, i, 16))
                bank = psB[:, c % 2, :]
                rows = slice(64 * e, 64 * e + 64)
                pe.matmul(bank[:, 0:keys], qh[:, e, n * P:(n + 1) * P], kh[:, e, 0:keys], start=True, stop=False)
                pe.matmul(bank[:, 0:keys], qrh[rows, e, n * P:(n + 1) * P], ropek[rows, 0:keys], start=False, stop=False)
                pe.matmul(bank[:, n * P:keys], ident, causal, start=False, stop=True).then_inc(m_s, 1)

            def mla_turn(c, i):
                h, n = divmod(c, TT)
                pe.wait_ge(m_w, at(c + 1, i, 16))
                if c >= 2:
                    pe.wait_ge(m_c, at(c - 1, i, 16))
                for kb in range(n + 1):
                    mm = pe.transpose(psB[:, 2 + c % 2, kb * P:(kb + 1) * P], mp[:, c % 2, kb * P:(kb + 1) * P], ident)
                mm.then_inc(m_t, 1)

            def mla_weigh(c, i):
                h, n = divmod(c, TT)
                e = h % 2
                t = TILE_AT["mhead"] + (63 if h == MLA_HEADS - 1 else 4 * h + 6)
                bank = psA[:, t % RING, :]
                if n == 0:
                    free_bank(t, i, 16)
                    pe.wait_ge(out_, at(TILE_AT["mhead"] + (3 if h == 0 else 4 * h + 2), i, 16))
                pe.wait_ge(m_c, at(c + 1, i, 16))
                for kb in range(n + 1):
                    mm = pe.matmul(bank[:, n * P:(n + 1) * P], vh[:, e, kb, :], mpT[:, c % 2, kb, :],
                                   start=(kb == 0), stop=(kb == n))
                mm.then_inc(done if n == TT - 1 else m_v, 1)

            def mla_head(h, i):
                for n in range(TT):
                    c = TT * h + n
                    if n < 3 and h + 1 < MLA_HEADS:
                        head_tile(n, h + 1, i)
                    mla_turn(c, i)
                    if c + 2 < TT * MLA_HEADS:
                        mla_scores(c + 2, i)
                    mla_weigh(c, i)

            for x in range(3):
                head_tile(x, 0, None)
            mla_scores(0, None)
            mla_scores(1, None)
            for h in range(4):
                mla_head(h, None)
            with pe.Fori(0, 2) as i:
                for h in range(4, 8):
                    mla_head(h, i)
            for h in range(12, 16):
                mla_head(h, None)
            pe.wait_ge(m_y, MLA_HEADS)
            project16("mout", (xx, mz_lo))
            pool_layer(1)
            norm("fin2")

        @block.scalar
        def _(act):
            def norm(name, src, meta=None):
                n, k0, kn = NORM_I[name], NORM_AT[name], NORM_K[name]
                for k in range(kn):
                    if k0 + k >= 2:
                        act.wait_ge(squ, k0 + k - 1)
                    if meta:
                        act.activation(sq[:, (k0 + k) % 2, T:TM], meta(k), ACT.Square)
                    act.activation(sq[:, (k0 + k) % 2, 0:T], src(k), ACT.Square).then_inc(sqr, 1)
                act.wait_ge(msr, n + 1)
                w = TM if meta else T
                act.activation(rt[:, 0:w], ms[:, 0:w], ACT.Abs_reciprocal_sqrt).then_inc(rtr, 1)
                for k in range(kn if name in SPLIT_AT else 0):
                    act.wait_ge(xsc, SPLIT_AT[name] + k + 1)
                    full, high = ((latn[:, k, :], lat_hi[:, k, :]) if name == "qlat" else
                                  (latn[:, QL + k, :], lat_hi[:, QL + k, :]) if name == "kvlat" else
                                  (xn[:, k, 0:w], xh[:, k, 0:w]))
                    act.activation(high, full, ACT.Copy).then_inc(xhi, 1)

            def take(dst, t, i=None, per=0, func=ACT.Copy, rows=P):
                act.wait_ge(done, at(t + 1, i, per))
                act.activation(dst, psA[0:rows, t % RING, :], func).then_inc(out_, 1)

            act.wait_ge(s_lam, 1)
            act.activation(lamc[:, 2:4], lamc[:, 0:2], ACT.Sigmoid)
            act.activation(lamc[:, 6:8], lamc[:, 0:2], ACT.Sigmoid, scale=-1.0).then_inc(s_lame, 1)
            act.wait_ge(s_lam, 2)
            act.activation(lb[:, 0:2, :], lb[:, 2:4, :], ACT.Sigmoid).then_inc(s_lame, 1)
            norm("mix", lambda k: hT[:, k, :], lambda k: hM[:, k, :])
            for name, dst, func, meta in (("ak", kraw, ACT.Copy, True), ("aq", qraw, ACT.Copy, False),
                                         ("rf", kk, ACT.Sigmoid, True), ("rq", q_rec, ACT.Silu, False),
                                         ("rg", gate, ACT.Silu, False)):
                for r in range(4):
                    if meta:
                        act.wait_ge(done, TILE_AT[name] + r + 1)
                        act.activation(dst[:, r, T:TM], psB[:, r, 0:M], func)
                    take(dst[:, r, 0:T], TILE_AT[name] + r, func=func)
            for name, dst in (("av", av), ("ri", ri)):
                for t in range(TT + 1):
                    rows = P if t < TT else M
                    take(dst[0:rows, t, :], TILE_AT[name] + t, rows=rows)

            def exps(n):
                lo = T - (n % TT + 1) * P
                act.wait_ge(a_m, n + 1)
                if n:
                    act.wait_ge(a_w, n)
                for p in range(2):
                    mm = act.activation(probs[:, p, lo:TM], psBf[:, 1024 * p + lo:1024 * p + TM], ACT.Exp,
                                        bias=nmax[:, p:p + 1], scale=0.125, accum_out=ssum[:, p:p + 1])
                mm.then_inc(a_p, 1)

            exps(0)
            for n in range(HEADS * TT):
                h, i = divmod(n, TT)
                act.wait_ge(a_t, n + 1)
                if n:
                    act.wait_ge(a_o, n)
                act.activation(wT[:, 0:i + 1, :], psA[:, 0, 0:(i + 1) * P].rearrange("p (a b) -> p a b", b=P), ACT.Copy)
                act.activation(wT[0:M, TT, :], psA[0:M, 1, 0:P], ACT.Copy).then_inc(a_c, 1)
                if n + 1 < HEADS * TT:
                    exps(n + 1)
                if i == TT - 1:
                    act.wait_ge(a_o, n + 1)
                    act.activation(mixed[:, h, :], psA[:, 2 + h % 2, :], ACT.Copy).then_inc(a_oc, 1)
            act.wait_ge(a_oc, HEADS)
            for h in range(HEADS):
                norm(f"att{h}", lambda k: mixed[:, h, :])

            act.wait_ge(s_f, 1)
            act.activation(cum, cum, ACT.Ln).then_inc(s_g, 1)
            act.wait_ge(g_d, 1)
            act.activation(qd, cum[:, :, 0:T], ACT.Exp).then_inc(g_e, 1)
            act.activation(el[:, :, 0:TT], cum[:, :, P - 1:T:P], ACT.Exp).then_inc(g_e, 1)
            act.wait_ge(g_d, 2)
            act.activation(kd, kd, ACT.Exp).then_inc(g_e, 1)
            for lv in range(GLA_LEVELS):
                act.wait_ge(g_d, 3 + lv)
                act.activation(lev[lv % 2], lev[lv % 2], ACT.Exp).then_inc(g_e, 1)
            for h in range(HEADS):
                act.wait_ge(g_t, h + 1)
                act.activation(kdT[:, h, 0:TT, :], psB[:, h % 2, :].rearrange("p (a b) -> p a b", b=P), ACT.Copy)
                act.activation(kdT[0:M, h, TT, :], psB[0:M, 2 + h % 2, 0:P], ACT.Copy).then_inc(g_k, 1)
            for h in range(HEADS):
                act.wait_ge(g_o, h + 1)
                act.activation(mixed[:, HEADS + h, :], psA[:, h, :], ACT.Copy).then_inc(g_oc, 1)
            act.wait_ge(g_oc, HEADS)
            for h in range(HEADS):
                norm(f"rec{h}", lambda k: mixed[:, HEADS + h, :])
            act.wait_ge(out_, TILE_AT["wo"] + 8)
            norm("ffn", lambda k: hT[:, k, :])

            with act.Fori(0, 4) as i:
                for r in range(4):
                    take(qp[:, bass.ds(i * 4 + r, 1), :].rearrange("p o n -> p (o n)"), TILE_AT["wq"] + r, i, 4)

            def take_scores(tt):
                for b in range(4):
                    take(sc[tt][:, 4 * b:4 * b + 4, :].rearrange("p a b -> p (a b)"), TILE_AT["sk"] + 4 * tt + b)

            def gate_exp(tt):
                act.wait_ge(p_ge, tt + 1)
                act.activation(gates, gates, ACT.Exp).then_inc(p_gx, 1)

            def take_slots(tt):
                act.wait_ge(p_tp, tt + 1)
                for x, dst in enumerate((it_, jt_, gt_)):
                    mm = act.activation(dst[:, tt * P:(tt + 1) * P], psB[:, tt % 2, x * P:(x + 1) * P], ACT.Copy)
                mm.then_inc(p_tc, 1)

            def early_gelu(u, i):
                if u >= 4:
                    act.wait_ge(p_hw[u % 4], at(16 * (u // 4), i, 16))
                take(early[u % 4], TILE_AT["early"] + u, i, 4, func=ACT.Gelu)

            for tt in range(TT):
                take_scores(tt)
            for tt in range(TT):
                if tt == 0:
                    for u in range(8):
                        early_gelu(u, None)
                else:
                    with act.Fori(0, 2) as i:
                        for r in range(4):
                            early_gelu(8 * tt + r, i)
                gate_exp(tt)
                take_slots(tt)

            def stages(t0, i):
                for t in (t0, t0 + 1):
                    if t >= 2:
                        act.wait_ge(p_gw[t % 2], at(32 * (t // 2), i, 32))
                    for c in range(STAGE // 4):
                        q = c % 4
                        act.wait_ge(p_om, at(STAGE // 4 * t + c + 1, i, STAGE // 2))
                        act.activation(stage[t % 2].rearrange("p g r t -> p (g r) t")[:, :, 4 * c:4 * c + 4]
                                       .rearrange("p j t -> p t j"),
                                       psB[:, q, :].rearrange("p (t j) -> p t j", j=P), ACT.Copy).then_inc(p_st, 1)
                        if q == 3:
                            u = EARLY // 2 + 4 * t + c // 4
                            act.wait_ge(p_hw[u % 4], at(16 * (u // 4), i, 32))
                            take(early[u % 4], TILE_AT["early"] + u, i, 8, func=ACT.Gelu)

            stages(0, None)
            with act.Fori(0, T // STAGE // 2 - 1) as i:
                stages(2, i)
            for b in range(2):
                act.wait_ge(p_gw[b], 16 * T // STAGE)

            def gelus(g, b, gi):
                if g >= 2:
                    act.wait_ge(p_y, at(8 * (g - 1), gi, 16))
                for x in range(2):
                    take(ge[:, b, 2 + x, :], TILE_AT["u"] + 2 * g + x, gi, 4, func=ACT.Gelu)

            gelus(0, 0, None)
            gelus(1, 1, None)
            with act.Fori(0, 15) as i:
                gelus(2, 0, i)
                gelus(3, 1, i)
            act.wait_ge(p_ya, 8 * 32)
            norm("fin1", lambda k: hT[:, k, :])

            def pool_layer(j):
                norm(f"pool{j}", lambda k: hT[:, k, :])
                t0 = TILE_AT[f"pin{j}"]
                act.wait_ge(u_a, j + 1)

                def turn(m0, i):
                    for c in range(2):
                        if m0 or i is not None:
                            act.wait_ge(u_p, at(16 * j + m0 + c - 1, i, 2))
                        take(upad[:, c, M:TM], t0 + 2 * (m0 + c), i, 4)
                        m = m0 + c if i is None else None
                        z = zb[:, m, :] if i is None else zb[:, bass.ds(i * 2 + m0 + c, 1), :].rearrange("p o n -> p (o n)")
                        take(z, t0 + 2 * (m0 + c) + 1, i, 4, func=ACT.Silu)

                turn(0, None)
                with act.Fori(0, 7) as i:
                    turn(2, i)

            act.wait_ge(xnr, NORM_AT["fin1"] + KD)
            pool_layer(0)
            act.wait_ge(out_, TILE_AT["pout0"] + 8)
            norm("conv", lambda k: hT[:, k, :])

            def conv_turn(m, i):
                if m:
                    act.wait_ge(c_y, at(m, i, 1))
                for x in range(4):
                    take(cbuf[:, x, :], TILE_AT["cin"] + 4 * m + x, i, 4, func=ACT.Silu if x == 3 else ACT.Copy)

            conv_turn(0, None)
            with act.Fori(0, 15) as i:
                conv_turn(1, i)
            act.wait_ge(out_, TILE_AT["cout"] + 8)
            norm("mla", lambda k: hT[:, k, :])
            with act.Fori(0, 4) as i:
                for r in range(4):
                    take(mz[:, bass.ds(i * 4 + r, 1), :].rearrange("p o n -> p (o n)"), TILE_AT["mz"] + r, i, 4, func=ACT.Silu)
            for r in range(6):
                take(lat[:, r, :], TILE_AT["mlat"] + r)
            act.wait_ge(out_, TILE_AT["mlat"] + 6)
            norm("qlat", lambda k: lat[:, k, :])
            norm("kvlat", lambda k: lat[:, QL + k, :])
            act.wait_ge(m_ang, 1)
            act.activation(sin2, sin2, ACT.Sin).then_inc(m_tab, 1)
            act.wait_ge(m_ang, 2)
            act.activation(cos2, cos2, ACT.Sin).then_inc(m_tab, 1)
            for t in range(8):
                take(qrope[:, t, :], TILE_AT["mqr"] + t)
            act.wait_ge(s_rope, 2 * HEADS + 9)

            def take_head(x, h, i):
                t = TILE_AT["mhead"] + (x if h == 0 else 4 * h - 1 + x)
                e = h % 2
                if x == 0:
                    rows = slice(64 * e, 64 * e + 64)
                    pair = (qrope[rows, h // 2, :] if i is None else
                            qrope[rows, bass.ds(i * 2 + h // 2, 1), :].rearrange("p o n -> p (o n)"))
                    act.activation(qrh[rows, e, :], pair, ACT.Copy)
                take((qh[:, e, :], kh[:, e, :], vh[:, e].rearrange("p a b -> p (a b)"))[x], t, i, 16)

            def mla_exp(c, i):
                keys = (c % TT + 1) * P
                act.wait_ge(m_m, at(c + 1, i, 16))
                if c >= 2:
                    act.wait_ge(m_t, at(c - 1, i, 16))
                act.activation(mp[:, c % 2, 0:keys], psB[:, c % 2, 0:keys], ACT.Exp, bias=mneg[:, c % 2:c % 2 + 1],
                               scale=MLA_SCALE, accum_out=msum[:, c % 2:c % 2 + 1]).then_inc(m_p, 1)

            def mla_head(h, i):
                for n in range(TT):
                    c = TT * h + n
                    if n < 3 and h + 1 < MLA_HEADS:
                        take_head(n, h + 1, i)
                    act.wait_ge(m_t, at(c + 1, i, 16))
                    if c >= 2 and n != 1:
                        act.wait_ge(m_v, at(3 * h + (0 if n == 0 else n - 1), i, 12))
                    act.activation(mpT[:, c % 2, 0:n + 1, :],
                                   psB[:, 2 + c % 2, 0:(n + 1) * P].rearrange("p (a b) -> p a b", b=P), ACT.Copy).then_inc(m_c, 1)
                    if c + 2 < TT * MLA_HEADS:
                        mla_exp(c + 2, i)
                if h >= 2:
                    act.wait_ge(m_y, at(h - 1, i, 4))
                take(obuf[:, h % 2, :], TILE_AT["mhead"] + (63 if h == MLA_HEADS - 1 else 4 * h + 6), i, 16)

            for x in range(3):
                take_head(x, 0, None)
            mla_exp(0, None)
            mla_exp(1, None)
            for h in range(4):
                mla_head(h, None)
            with act.Fori(0, 2) as i:
                for h in range(4, 8):
                    mla_head(h, i)
            for h in range(12, 16):
                mla_head(h, None)
            act.wait_ge(out_, TILE_AT["mout"] + 8)
            pool_layer(1)
            act.wait_ge(out_, TILE_AT["pout1"] + 8)
            norm("fin2", lambda k: hT[:, k, :])

        @block.vector
        def _(dve):
            step = Steps(dve, own)

            def norm(name, src, dst, g, meta=False, width=D):
                n, k0, kn = NORM_I[name], NORM_AT[name], NORM_K[name]
                dve.wait_ge(squ, k0 + kn)
                w = T
                if meta:
                    w = TM
                    dve.tensor_scalar(ms[:, T:TM], psB[:, 2, 0:M], 1.0 / width, EPS, ALU.mult, ALU.add)
                dve.tensor_scalar(ms[:, 0:T], psB[:, 3, :], 1.0 / width, EPS, ALU.mult, ALU.add).then_inc(msr, 1)
                dve.wait_ge(rtr, n + 1)
                if n:
                    dve.wait_ge(xnr, k0)
                step(dve.scalar_tensor_tensor(newt[:, 0:w], rt[:, 0:w], -0.5, rt[:, 0:w], ALU.mult, ALU.mult))
                step.wait()
                step(dve.tensor_tensor(newt[:, 0:w], newt[:, 0:w], ms[:, 0:w], ALU.mult))
                step.wait()
                step(dve.scalar_tensor_tensor(rstd[:, 0:w], newt[:, 0:w], 1.5, rt[:, 0:w], ALU.add, ALU.mult))
                step.wait()
                wide = name in SPLIT_AT

                def lo(k):
                    dve.wait_ge(xhi, SPLIT_AT[name] + k + 1)
                    full, low, high = (v[:, k, :] if name == "qlat" else v[:, QL + k, :] if name == "kvlat" else v[:, k, 0:w]
                                       for v in ((latn, lat_lo, lat_hi) if name.endswith("lat") else (xn, xlo, xh)))
                    dve.tensor_tensor(low, full, high.bitcast(F32), ALU.subtract).then_inc(xnr, 1)

                for k in range(kn):
                    if meta:
                        dve.scalar_tensor_tensor(xn[:, k, T:TM], hM[:, k, :], g(k), rstd[:, T:TM], ALU.mult, ALU.mult)
                    dve.scalar_tensor_tensor(dst(k), src(k), g(k), rstd[:, 0:T], ALU.mult, ALU.mult).then_inc(xsc if wide else xnr, 1)
                    if wide and k:
                        lo(k - 1)
                if wide:
                    lo(kn - 1)

            def norm_stream(name, dst=None):
                norm(name, lambda k: hT[:, k, :], dst or (lambda k: xn[:, k, 0:T]), lambda k: pcol(name, k))

            def add_tiles(name):
                t0 = TILE_AT[name]
                with dve.Fori(0, 2) as i:
                    for r in range(4):
                        dve.wait_ge(done, at(t0 + r + 1, i, 4))
                        h = hT[:, bass.ds(i * 4 + r, 1), :].rearrange("p o n -> p (o n)")
                        dve.tensor_tensor(h, h, psA[:, (t0 + r) % RING, :], ALU.add).then_inc(out_, 1)

            dve.wait_ge(s_in, 64)
            lam = pcol("lam", 0, 256).rearrange("p (a b c) -> p a b c", a=2, b=2)
            step(dve.tensor_tensor(lamp, lam[:, :, 0, :], lam[:, :, 1, :], ALU.mult))
            step.wait()
            dve.tensor_reduce(lamc[:, 0:2], lamp, AX_X, ALU.add).then_inc(s_lam, 1)
            step(dve.tensor_tensor(lb[:, 2, :], pcol("lb0", 0, 4), pcol("lb1", 0, 4), ALU.subtract))
            dve.tensor_tensor(lb[:, 3, :], pcol("lb1", 0, 4), pcol("lb0", 0, 4), ALU.subtract).then_inc(s_lam, 1)
            dve.wait_ge(s_lame, 1)
            step(dve.reciprocal(lamc[:, 6:8], lamc[:, 6:8]))
            step.wait()
            step(dve.tensor_tensor(lamc[:, 2:4], lamc[:, 2:4], lamc[:, 6:8], ALU.mult))
            step.wait()
            step(dve.scalar_tensor_tensor(lamc[:, 4:5], lamc[:, 2:3], LAM_INIT, lamc[:, 3:4], ALU.add, ALU.subtract))
            step(dve.tensor_scalar(lamc[:, 5:6], pcol("att"), 1.0 - LAM_INIT, None, ALU.mult))
            dve.wait_ge(s_lame, 2)

            norm("mix", lambda k: hT[:, k, :], lambda k: xn[:, k, 0:T], lambda k: pcol("mix", k), meta=True)

            dve.wait_ge(out_, TILE_AT["rf"] + 4)
            for h in range(HEADS):
                step(dve.tensor_scalar(cum[:, h, :], kk[:, h, :], lb[:, 1, h:h + 1], lb[:, 0, h:h + 1], ALU.mult, ALU.add))
            step.wait()
            dve.tensor_scalar(kk, cum, -1.0, 1.0, ALU.mult, ALU.add).then_inc(s_f, 1)
            dve.wait_ge(s_tab, 32)
            for j in range(2 * HEADS):
                dve.wait_ge(s_perm, j + 1)
                if j:
                    dve.wait_ge(s_rope, j)
                raw, dst, h, w = (kraw, kT, j, TM) if j < HEADS else (qraw, qT, j - HEADS, T)
                if j < HEADS:
                    step(dve.tensor_tensor(ropt[:, T:TM], psB[:, 2 + j % 2, 0:M], sinA[:, T:TM], ALU.mult))
                step(dve.tensor_tensor(ropt[:, 0:T], psB[:, j % 2, :], sinA[:, 0:T], ALU.mult))
                step(dve.tensor_tensor(dst[:, h, 0:w], raw[:, h, 0:w], cosA[:, 0:w], ALU.mult))
                step.wait()
                dve.tensor_tensor(dst[:, h, 0:w], dst[:, h, 0:w], ropt[:, 0:w], ALU.add).then_inc(s_rope, 1)

            pair = psB[:, :, :].rearrange("p (a b) n -> p a (b n)", a=2)

            def maxima(n):
                lo = T - (n % TT + 1) * P
                dve.wait_ge(a_s, n + 1)
                step(dve.tensor_reduce(smax, pair[:, :, lo:TM], AX_X, ALU.max))
                step.wait()
                dve.tensor_scalar(nmax, smax, -0.125, None, ALU.mult).then_inc(a_m, 1)

            maxima(0)
            for n in range(HEADS * TT):
                lo = T - (n % TT + 1) * P
                dve.wait_ge(a_p, n + 1)
                if n:
                    dve.wait_ge(a_w, n)
                step(dve.reciprocal(rsum, ssum))
                step.wait()
                step(dve.tensor_tensor(rsum[:, 1:2], rsum[:, 1:2], lamc[:, 4:5], ALU.mult))
                step.wait()
                step(dve.tensor_scalar(probs[:, 1, lo:TM], probs[:, 1, lo:TM], rsum[:, 1:2], None, ALU.mult))
                step.wait()
                if n:
                    dve.wait_ge(a_t, n)
                dve.scalar_tensor_tensor(wgt[:, lo:TM], probs[:, 0, lo:TM], rsum[:, 0:1], probs[:, 1, lo:TM],
                                         ALU.mult, ALU.subtract).then_inc(a_w, 1)
                if n + 1 < HEADS * TT:
                    maxima(n + 1)
            for h in range(HEADS):
                norm(f"att{h}", lambda k: mixed[:, h, :], lambda k: mixed[:, h, :], lambda k: lamc[:, 5:6], width=P)

            dve.wait_ge(s_g, 1)
            dve.wait_ge(s_tab3, 32)
            cflat = cum.rearrange("p h t -> p (h t)")
            dve.tensor_tensor_scan(cflat, reset, cflat, 0.0, ALU.mult, ALU.add).then_inc(g_d, 1)
            dve.wait_ge(g_d, 1)
            creal = cum[:, :, 0:T].rearrange("p h (c t) -> p h c t", t=P)
            last = creal[:, :, :, P - 1:P].to_broadcast([P, HEADS, TT, P])
            step(dve.tensor_tensor(kd[:, :, 0:T].rearrange("p h (c t) -> p h c t", t=P), last, creal, ALU.subtract))
            dve.tensor_tensor(kd[:, :, T:TM], cum[:, :, TM - 1:TM].to_broadcast([P, HEADS, M]), cum[:, :, T:TM],
                              ALU.subtract).then_inc(g_d, 1)
            step(dve.memset(pairT, 0.0))

            def halves(x, half):
                v = x.rearrange("p h (b t) -> p h b t", t=2 * half)
                return v[:, :, :, 0:half], v[:, :, :, half:2 * half]

            def difference(lv):
                half = P >> (lv + 1)
                lo, hi = halves(cum[:, :, 0:T], half)
                mid = lo[:, :, :, half - 1:half].to_broadcast([P, HEADS, T // (2 * half), half])
                dlo, dhi = halves(lev[lv % 2], half)
                step(dve.tensor_tensor(dlo, mid, lo, ALU.subtract))
                dve.tensor_tensor(dhi, hi, mid, ALU.subtract).then_inc(g_d, 1)

            difference(0)
            difference(1)
            for lv in range(GLA_LEVELS + 1):
                if lv < GLA_LEVELS:
                    half = P >> (lv + 1)
                    dve.wait_ge(g_e, 4 + lv)
                    dlo, dhi = halves(lev[lv % 2], half)
                    step(dve.tensor_tensor(dlo, dlo, halves(kk[:, :, 0:T], half)[0], ALU.mult))
                    dve.tensor_tensor(dhi, dhi, halves(q_rec, half)[1], ALU.mult).then_inc(g_l, 1)
                if lv == 0:
                    step(dve.tensor_tensor(qd, qd, q_rec, ALU.mult))
                    dve.tensor_tensor(kd, kd, kk, ALU.mult).then_inc(g_q, 1)
                    step.wait()
                for v in ([lv - 1] if lv else []) + ([lv] if lv == GLA_LEVELS else []):
                    mask = lgm[:, v, :].bitcast(U32).unsqueeze(1).to_broadcast([P, TT, P])
                    for h in range(HEADS):
                        dve.wait_ge(g_a, HEADS * v + h + 1)
                        if v:
                            dve.wait_ge(g_c, HEADS * (v - 1) + h + 1)
                        dve.copy_predicated(pairT[:, h, :].rearrange("p (c t) -> p c t", t=P), mask,
                                            psA[:, h, :].rearrange("p (c t) -> p c t", t=P)).then_inc(g_c, 1)
                if 1 <= lv < GLA_LEVELS - 1:
                    difference(lv + 1)
            dve.wait_ge(g_u, 1)
            dve.tensor_copy(state[:, 0].rearrange("p h v -> p (h v)"), psB[:, 0, :]).then_inc(g_s, 1)
            for n in range(1, TT):
                dve.wait_ge(g_u, n + 1)
                dve.wait_ge(g_s, n)
                for h in range(HEADS):
                    ins = dve.scalar_tensor_tensor(state[:, n, h, :], state[:, n - 1, h, :], el[:, h, n - 1:n],
                                                   psB[:, n % 2, h * P:(h + 1) * P], ALU.mult, ALU.add)
                ins.then_inc(g_s, 1)
            for h in range(HEADS):
                norm(f"rec{h}", lambda k: mixed[:, HEADS + h, :], lambda k: mixed[:, HEADS + h, :],
                     lambda k: pcol("rec", h), width=P)
                dve.wait_ge(xnr, NORM_AT[f"rec{h}"] + 1)
                dve.tensor_tensor(mixed[:, HEADS + h, :], mixed[:, HEADS + h, :], gate[:, h, :], ALU.mult).then_inc(n_m, 1)
                if h == 0:
                    dve.wait_ge(g_c, HEADS * (GLA_LEVELS + 1))
                dve.wait_ge(n_m, h + 1)
                for x in (h, HEADS + h):
                    step(dve.tensor_copy(xh[:, x, 0:T], mixed[:, x, :]))
                step.wait()
                for x in (h, HEADS + h):
                    dve.tensor_tensor(mixed_lo[:, x, :], mixed[:, x, :], xh[:, x, 0:T].bitcast(F32), ALU.subtract).then_inc(m_h, 1)
            add_tiles("wo")
            dve.wait_ge(out_, TILE_AT["wo"] + 8)
            norm_stream("ffn")

            siu = si.bitcast(U32)
            pos = posu.bitcast(U32)
            ab = abu.bitcast(U32)

            def best16(rows):
                first, cut, second = [], [], []
                for row, rest, best, where in rows:
                    first.append(step(dve.max(best[:, 0:8], row)))
                for x, (row, rest, best, where) in enumerate(rows):
                    step.wait(first[x])
                    cut.append(step(dve.match_replace(rest, best[:, 0:8], row, -3e38)))
                for row, rest, best, where in rows:
                    step(dve.max_index(where[:, 0:8], best[:, 0:8], row))
                for x, (row, rest, best, where) in enumerate(rows):
                    step.wait(cut[x])
                    second.append(step(dve.max(best[:, 8:16], rest)))
                for x, (row, rest, best, where) in enumerate(rows):
                    step.wait(second[x])
                    step(dve.max_index(where[:, 8:16], best[:, 8:16], rest))

            for tt in range(TT):
                dve.wait_ge(out_, TILE_AT["sk"] + 4 * tt + 4)
                for hp in range(0, 2 * PEER_HEADS, 2):
                    best16([(sc[tt][:, hp + x, :], sc2[:, x, :], sv[:, hp + x, :], siu[:, hp + x, :]) for x in range(2)])
                step.wait()
                step(dve.tensor_copy(sif, siu))
                sv4 = sv.rearrange("p (h x) k -> p h x k", x=2)
                step(dve.tensor_tensor(cand.rearrange("p h (a b) -> p h a b", a=TOPK),
                                       sv4[:, :, 0, :].unsqueeze(3).to_broadcast([P, PEER_HEADS, TOPK, TOPK]),
                                       sv4[:, :, 1, :].unsqueeze(2).to_broadcast([P, PEER_HEADS, TOPK, TOPK]), ALU.add))
                step.wait()
                for h in range(0, PEER_HEADS, 2):
                    best16([(cand[:, h + x, :], cand2[:, x, :], tops[:, h + x, :], pos[:, h + x, :]) for x in range(2)])
                if tt:
                    dve.wait_ge(p_tp, tt)
                step.wait()
                dve.tensor_tensor(gates, tops, tops[:, :, 0:1].to_broadcast([P, PEER_HEADS, TOPK]),
                                  ALU.subtract).then_inc(p_ge, 1)
                flat = pos.rearrange("p h k -> p (h k)")
                step(dve.tensor_scalar(ab[:, 0, :], flat, 4, None, ALU.logical_shift_right))
                step(dve.tensor_scalar(ab[:, 1, :], flat, 15, None, ALU.bitwise_and))
                step.wait()
                step(dve.tensor_copy(abf, ab))
                step.wait()
                sif4 = sif.rearrange("p (h x) k -> p h x k", x=2)
                for x in range(2):
                    step.wait()
                    step(dve.tensor_tensor(hot, abf[:, x, :].unsqueeze(2).to_broadcast([P, SLOTS, TOPK]),
                                           iota[:, 0:TOPK].unsqueeze(1).to_broadcast([P, SLOTS, TOPK]), ALU.is_equal))
                    step.wait()
                    hot4 = hot.rearrange("p (h k) a -> p h k a", k=TOPK)
                    step(dve.tensor_tensor(hot4, hot4, sif4[:, :, x, :].unsqueeze(2).to_broadcast(
                        [P, PEER_HEADS, TOPK, TOPK]), ALU.mult))
                    step.wait()
                    step(dve.tensor_reduce(sel[:, x, :], hot, AX_X, ALU.add))
                dve.wait_ge(p_gx, tt + 1)
                step(dve.tensor_reduce(gsum, gates, AX_X, ALU.add))
                step.wait()
                step(dve.reciprocal(gsum, gsum))
                step.wait()
                dve.tensor_tensor(gates, gates, gsum.unsqueeze(2).to_broadcast([P, PEER_HEADS, TOPK]),
                                  ALU.mult).then_inc(p_x, 1)
                dve.wait_ge(p_x, tt + 1)

            def onehots(n0, i):
                for q in range(4):
                    if n0 + q >= 4:
                        dve.wait_ge(p_om, at(n0 + q - 3, i, 4))
                    for u in range(4):
                        token = 4 * (n0 + q) + u
                        c = slice(token, token + 1) if i is None else bass.ds(i * 16 + token, 1)
                        b = 4 * q + u
                        dve.tensor_scalar(oneI[:, b, :], iota, it_[:, c], gt_[:, c], ALU.is_equal, ALU.mult)
                        ins = dve.tensor_scalar(oneJ[:, b, :], iota, jt_[:, c], None, ALU.is_equal)
                    ins.then_inc(p_oh, 1)

            dve.wait_ge(p_tc, TT)
            onehots(0, None)
            with dve.Fori(0, 31) as i:
                onehots(4, i)

            def gated(g, b, gi):
                dve.wait_ge(p_g[b], at(16 * (g // 2 + 1), gi, 16))
                dve.wait_ge(p_hl[b], at(16 * (g // 2 + 1), gi, 16))
                for r in range(4):
                    if r >= 2:
                        dve.wait_ge(out_, at(TILE_AT["u"] + 2 * g + r - 1, gi, 4))
                    weight = ge[:, b, r, :].rearrange("p (t n) -> p t n", n=STAGE)
                    step(dve.tensor_tensor(weight, weight, gbuf[:, b, :, r, :], ALU.mult))
                    step.wait()
                    step(dve.tensor_copy(ghi[:, b, :, r, :], weight))
                    step.wait()
                    dve.tensor_tensor(glo[:, b, r, :].rearrange("p (t n) -> p t n", n=STAGE), weight,
                                      ghi[:, b, :, r, :].bitcast(F32), ALU.subtract).then_inc(p_w, 1)

            def add_out(g, gi):
                for d in range(KD):
                    dve.wait_ge(p_y, at(8 * g + d + 1, gi, 16))
                    dve.tensor_tensor(hT[:, d, :], hT[:, d, :], psB[:, d % 4, :], ALU.add).then_inc(p_ya, 1)

            gated(0, 0, None)
            gated(1, 1, None)
            add_out(0, None)
            gated(2, 0, None)
            add_out(1, None)
            with dve.Fori(0, 14) as i:
                step.enter(i, 16)
                gated(3, 1, i)
                add_out(2, i)
                gated(4, 0, i)
                add_out(3, i)
                step.leave(14)
            gated(31, 1, None)
            add_out(30, None)
            add_out(31, None)
            norm_stream("fin1", lambda k: hT[:, k, :])

            def pool_layer(j):
                step(dve.memset(win[0][:, 0:M], 0.0))
                step(dve.memset(win[1][:, 0:M], 0.0))
                dve.memset(upad[:, :, 0:M], 0.0).then_inc(u_a, 1)
                norm_stream(f"pool{j}")
                dve.wait_ge(s_tab2, 16 if j == 0 else 48)
                t0 = TILE_AT[f"pin{j}"]
                for g in range(len(WINDOWS)):
                    with dve.Fori(0, 2) as i:
                        step.enter(i, 2 * (g + 4))
                        for c in range(2):
                            m = 4 * g + c
                            dve.wait_ge(out_, at(t0 + 2 * m + 1, i, 4))
                            u = src = upad[:, c, :]
                            for x in range(g + 1):
                                dst = win[x % 2]
                                step(dve.tensor_tensor(dst[:, M:TM], src[:, M:TM], src[:, M - (1 << x):TM - (1 << x)], ALU.add))
                                step.wait()
                                src = dst
                            low, high = (v[:, bass.ds(i * 2 + m, 1), :].rearrange("p o n -> p (o n)") for v in (pooled, pooledh))
                            step(dve.scalar_tensor_tensor(ptmp, src[:, M:TM], 1.0 / WINDOWS[g], u[:, M:TM], ALU.mult, ALU.subtract))
                            step(dve.tensor_tensor(pfew, src[:, M:2 * M], rcnt[:, g, :], ALU.mult))
                            step.wait()
                            dve.tensor_tensor(ptmp[:, 0:M], pfew, u[:, M:2 * M], ALU.subtract).then_inc(u_f, 1)
                            dve.wait_ge(u_f, at(16 * j + m + 1, i, 2))
                            step(dve.tensor_copy(high, ptmp))
                            step.wait()
                            dve.tensor_tensor(low, ptmp, high.bitcast(F32), ALU.subtract).then_inc(u_p, 1)
                            dve.wait_ge(u_p, at(16 * j + m + 1, i, 2))
                        step.leave(2)
                name = f"pgrp{j}"
                t0 = TILE_AT[name]
                dve.wait_ge(out_, t0)
                with dve.Fori(0, 4) as i:
                    step.enter(i, 4)
                    for r in range(4):
                        dve.wait_ge(done, at(t0 + r + 1, i, 4))
                        z = zb[:, bass.ds(i * 4 + r, 1), :].rearrange("p o n -> p (o n)")
                        dve.scalar_tensor_tensor(z, psA[:, (t0 + r) % RING, :],
                                                 par[:, bass.ds(i * 4 + (PAR_AT[f"pscale{j}"] + r), 1)], z,
                                                 ALU.mult, ALU.mult).then_inc(out_, 1)
                        dve.wait_ge(out_, at(t0 + r + 1, i, 4))
                        high = xx[:, bass.ds(i * 4 + r, 1), 0:T].rearrange("p o n -> p (o n)")
                        step(dve.tensor_copy(high, z))
                        step.wait()
                        dve.tensor_tensor(zb_lo[:, bass.ds(i * 4 + r, 1), :].rearrange("p o n -> p (o n)"), z,
                                          high.bitcast(F32), ALU.subtract).then_inc(z_h, 1)
                    step.leave(4)
                add_tiles(f"pout{j}")
                dve.wait_ge(out_, TILE_AT[f"pout{j}"] + 8)

            dve.wait_ge(xnr, NORM_AT["fin1"] + KD)
            pool_layer(0)

            step(dve.memset(chpad[:, 0:2], 0.0))
            norm_stream("conv")

            def conv_w(k, m, i):
                c = PAR_AT["convw"] + 16 * k + m
                return par[:, c:c + 1] if i is None else par[:, bass.ds(i + c, 1)]

            with dve.Fori(0, 16) as i:
                step.enter(i, 7)
                t0 = TILE_AT["cin"]
                c, h, b, z = (cbuf[:, x, :] for x in range(4))
                dve.wait_ge(out_, at(t0 + 2, i, 4))
                step(dve.tensor_tensor(chpad[:, 2:T + 2], c, h, ALU.mult))
                step.wait()
                step(dve.tensor_scalar(cacc[:, 0, :], chpad[:, 0:T], conv_w(0, 0, i), None, ALU.mult))
                step.wait()
                step(dve.scalar_tensor_tensor(cacc[:, 1, :], chpad[:, 1:T + 1], conv_w(1, 0, i), cacc[:, 0, :], ALU.mult, ALU.add))
                step.wait()
                step(dve.scalar_tensor_tensor(cacc[:, 0, :], chpad[:, 2:T + 2], conv_w(2, 0, i), cacc[:, 1, :], ALU.mult, ALU.add))
                step.wait()
                dve.wait_ge(out_, at(t0 + 3, i, 4))
                step(dve.tensor_tensor(cacc[:, 1, :], cacc[:, 0, :], b, ALU.mult))
                step.wait()
                dve.wait_ge(out_, at(t0 + 4, i, 4))
                step(dve.tensor_tensor(cacc[:, 0, :], cacc[:, 1, :], z, ALU.mult))
                step.wait()
                low, high = (v[:, bass.ds(i, 1), :].rearrange("p o n -> p (o n)") for v in (yb, yh))
                step(dve.tensor_copy(high, cacc[:, 0, :]))
                step.wait()
                dve.tensor_tensor(low, cacc[:, 0, :], high.bitcast(F32), ALU.subtract).then_inc(c_y, 1)
                dve.wait_ge(c_y, i + 1)
                step.leave(16)
            add_tiles("cout")
            dve.wait_ge(out_, TILE_AT["cout"] + 8)

            norm_stream("mla")
            dve.wait_ge(s_tab2, 32)
            step(dve.tensor_copy(ang, posi.bitcast(I32)))
            step.wait()
            freq = const[:, CONST_AT["invfreq"]:CONST_AT["invfreq"] + 1]
            step(dve.tensor_scalar(ang, ang, freq, None, ALU.mult))
            step.wait()
            turn = 2.0 * math.pi
            c1 = 6.28125
            c2 = float(np.float32(np.round((turn - c1) * 2.0 ** 20) / 2.0 ** 20))
            c3 = turn - c1 - c2
            magic = 1.5 * 2.0 ** 23
            for dst, quarter in ((sin2, 0.0), (cos2, 0.25)):
                step(dve.tensor_scalar(rn, ang, 1.0 / turn, quarter, ALU.mult, ALU.add))
                step.wait()
                step(dve.tensor_scalar(rn, rn, magic, None, ALU.add))
                step.wait()
                step(dve.tensor_scalar(rn, rn, magic, None, ALU.subtract))
                step.wait()
                src = ang
                for c in (c1, c2, c3):
                    step(dve.scalar_tensor_tensor(dst, rn, -c, src, ALU.mult, ALU.add))
                    step.wait()
                    src = dst
                step(dve.tensor_scalar(dst, dst, quarter * turn, None, ALU.add))
                step.wait()
                dve.tensor_scalar(dst, dst, 3.1415925, -3.1415925, ALU.min, ALU.max).then_inc(m_ang, 1)
            norm("qlat", lambda k: lat[:, k, :], lambda k: latn[:, k, :], lambda k: pcol("qlat", k), width=QL * P)
            norm("kvlat", lambda k: lat[:, QL + k, :], lambda k: latn[:, QL + k, :], lambda k: pcol("kvlat", k), width=KL * P)
            dve.wait_ge(m_tab, 2)
            sign = const[:, CONST_AT["sign"]:CONST_AT["sign"] + 1]
            step(dve.tensor_scalar(sin2, sin2, sign, None, ALU.mult))
            step.wait()
            for t in range(-1, 8):
                dve.wait_ge(s_perm, 2 * HEADS + t + 2)
                dve.wait_ge(s_rope, 2 * HEADS + t + 1)
                raw = lat[:, QL + KL, :] if t < 0 else qrope[:, t, :]
                dst = ropek if t < 0 else raw
                step(dve.tensor_tensor(rn, psB[:, (t + 1) % 2, :], sin2, ALU.mult))
                step(dve.tensor_tensor(dst, raw, cos2, ALU.mult))
                step.wait()
                dve.tensor_tensor(dst, dst, rn, ALU.add).then_inc(s_rope, 1)

            def mla_max(c, i):
                keys = (c % TT + 1) * P
                x = c % 2
                dve.wait_ge(m_s, at(c + 1, i, 16))
                step(dve.tensor_reduce(mmax[:, x:x + 1], psB[:, x, 0:keys], AX_X, ALU.max))
                step.wait()
                dve.tensor_scalar(mneg[:, x:x + 1], mmax[:, x:x + 1], -MLA_SCALE, None, ALU.mult).then_inc(m_m, 1)

            def mla_gate(h, i):
                t = TILE_AT["mhead"] + (63 if h == MLA_HEADS - 1 else 4 * h + 6)
                dve.wait_ge(out_, at(t + 1, i, 16))
                z, low, high = ((v[:, h, 0:T] if i is None else v[:, bass.ds(i * 4 + h, 1), 0:T].rearrange("p o n -> p (o n)"))
                                for v in (mz, mz_lo, xx))
                step(dve.tensor_tensor(z, obuf[:, h % 2, :], z, ALU.mult))
                step.wait()
                step(dve.tensor_copy(high, z))
                step.wait()
                dve.tensor_tensor(low, z, high.bitcast(F32), ALU.subtract).then_inc(m_y, 1)

            def mla_head(h, i):
                for n in range(TT):
                    c = TT * h + n
                    x, keys = c % 2, (n + 1) * P
                    dve.wait_ge(m_p, at(c + 1, i, 16))
                    step(dve.reciprocal(mrec[:, x:x + 1], msum[:, x:x + 1]))
                    step.wait()
                    dve.tensor_scalar(mp[:, x, 0:keys], mp[:, x, 0:keys], mrec[:, x:x + 1], None,
                                      ALU.mult).then_inc(m_w, 1)
                    if c + 2 < TT * MLA_HEADS:
                        mla_max(c + 2, i)
                    if n == 1 and h:
                        mla_gate(h - 1, i)

            mla_max(0, None)
            mla_max(1, None)
            for h in range(4):
                mla_head(h, None)
            with dve.Fori(0, 2) as i:
                step.enter(i, 40)
                for h in range(4, 8):
                    mla_head(h, i)
                step.leave(2)
            for h in range(12, 16):
                mla_head(h, None)
            mla_gate(15, None)
            add_tiles("mout")
            dve.wait_ge(out_, TILE_AT["mout"] + 8)
            pool_layer(1)
            norm_stream("fin2")


def _tiles(w):
    k, n = w.shape
    return w.reshape(k // P, P, n // P, P).transpose(2, 1, 0, 3)


def _slabs(tiles):
    n, _, k, _ = tiles.shape
    flat = tiles.transpose(0, 2, 1, 3).reshape(n * k, P, P)
    return flat.reshape(n * k // 8, 8, P, P).transpose(0, 2, 1, 3).reshape(-1, P, SLAB)


def _columns(v):
    return np.asarray(v).reshape(-1, P).T


def _constants():
    p = np.arange(P)
    rot = np.zeros((P, P), np.float32)
    rot[p // 64 * 64 + (p % 64 + 32) % 64, p] = 1.0
    causal = np.where(p[None, :] <= p[:, None], 0.0, BIG_NEG).astype(np.float32)
    iota = np.broadcast_to(p.astype(np.float32), (P, P))
    freq = (np.float32(10000.0) ** (-(np.arange(0, 64, 2, dtype=np.float32)) / np.float32(64))).astype(np.float32)
    sign = np.where(p % 64 < 32, -1.0, 1.0).astype(np.float32)
    const = np.concatenate([np.eye(P, dtype=np.float32), rot, causal, iota, freq[p % 32][:, None], sign[:, None]], axis=1)
    ang = (np.concatenate([np.arange(M, TM), np.arange(M)]).astype(np.float32)[None, :] * freq[p % 32][:, None]).astype(np.float32)
    cos, sin = np.cos(ang.astype(np.float64)), np.sin(ang.astype(np.float64)) * sign[:, None]
    s, t = p[:, None], p[None, :]
    levels = np.zeros((P, GLA_LEVELS + 1, P), np.float32)
    for lv in range(GLA_LEVELS):
        bit = P >> (lv + 1)
        levels[:, lv, :] = (s // (2 * bit) == t // (2 * bit)) & (s % (2 * bit) < bit) & (t % (2 * bit) >= bit)
    levels[:, GLA_LEVELS, :] = s == t
    reset = np.ones((HEADS, TM), np.float32)
    reset[:, 0:TM:P] = 0.0
    reset = np.broadcast_to(reset.reshape(-1), (P, HEADS * TM))
    count = np.arange(1, T + 1, dtype=np.float32)
    counts = np.broadcast_to(np.stack([1.0 / np.minimum(count, w) for w in WINDOWS]).astype(np.float32)[:, 0:M], (P, 4, M))
    f = np.ascontiguousarray
    return dict(const=f(const), cosA=f(cos, dtype=np.float32), sinA=f(sin, dtype=np.float32), levels=f(levels),
                reset=f(reset), counts=f(counts))


def _layout(x):
    f = np.ascontiguousarray
    w_in = x["w_in"][0]
    part = {}
    for name, c in zip(("aq", "ak", "av", "rq", "rf", "ri", "rg"), range(0, 7 * 512, 512)):
        part[name] = w_in[:, c:c + 512]
    rows = {n: part[n].reshape(4, 2, P, 512).transpose(0, 2, 1, 3).reshape(4, P, SLAB) for n in ("av", "ri")}
    sub = x["peer_subkeys"][0].reshape(2, 8, KEYS, P).transpose(0, 3, 1, 2).reshape(2, P, SLAB)
    w1 = np.concatenate([_slabs(_tiles(part[n])) for n in ("ak", "aq", "rf", "rq", "rg")] +
                        [rows["av"], rows["ri"], _slabs(_tiles(x["w_out"][0])), _slabs(_tiles(x["peer_w_query"][0])), sub])
    u = x["peer_u"][0].reshape(P, KEYS // 4, 2, 2, KD, P).transpose(2, 1, 3, 5, 4, 0).reshape(KEYS, P, SLAB)
    v = x["peer_v"][0].reshape(P, KEYS // 4, 4, D).transpose(1, 0, 2, 3).reshape(KEYS // 4, P, 4 * D)

    def pool(j):
        w = _tiles(x["pool_w_in_2"][j])
        w = np.stack([w[0:KI], w[KI:]], axis=1).reshape(2 * KI, P, KD, P)
        grp = np.concatenate([_tiles(g) for g in x["pool_w_grp_2"][j]])
        return [_slabs(w), _slabs(grp), _slabs(_tiles(x["pool_w_out_2"][j]))]

    c = _tiles(x["conv_w_in_2"][0]).reshape(4, KI, P, KD, P)
    conv = [_slabs(np.stack([c[1], c[2], c[0], c[3]], axis=1).reshape(4 * KI, P, KD, P)),
            _slabs(_tiles(x["conv_w_out_2"][0]))]
    w = x["mla_w_in_2"][0]
    kr = w[:, 640:704]
    qup = x["mla_w_q_up_2"][0].reshape(QL * P, MLA_HEADS, 192)
    kvup = x["mla_w_kv_up_2"][0].reshape(KL * P, MLA_HEADS, 256)
    heads = []
    for h in range(MLA_HEADS):
        t = np.concatenate([qup[:, h, 0:P].reshape(QL, P, P), kvup[:, h, 0:P].reshape(KL, P, P),
                            kvup[:, h, P:].reshape(KL, P, P), np.zeros((1, P, P), np.float32)])
        heads.append(t.transpose(1, 0, 2).reshape(P, SLAB))
    mla = [_slabs(_tiles(w[:, 704:])), _slabs(_tiles(np.concatenate([w[:, 0:640], kr, kr], axis=1))),
           _slabs(_tiles(qup[:, :, P:].reshape(QL * P, MLA_HEADS * 64))), np.stack(heads),
           _slabs(_tiles(x["mla_w_out_2"][0]))]
    w2 = np.concatenate(pool(0) + conv + mla + pool(1))
    par = [_columns(x[n].reshape(-1)) for n in ("mix_norm_w", "ffn_norm_w", "final_norm_w")]
    par += [_columns(x["pool_norm_2"][0]), _columns(x["pool_norm_2"][1])]
    par += [_columns(x[n].reshape(-1)) for n in ("conv_norm_2", "mla_norm_2", "final_norm_2", "mla_q_norm_2", "mla_kv_norm_2")]
    par += [_columns(x["pool_scale_2"][0]), _columns(x["pool_scale_2"][1]), _columns(x["conv_w_2"].reshape(-1)),
            _columns(x["rec_lb_logits"][0]), _columns(x["rec_lb_logits"][1]), _columns(x["rec_norm_w"].reshape(-1)),
            _columns(x["diff_subln_w"].reshape(-1))]
    lam = np.concatenate([x[n].reshape(-1) for n in ("diff_lambda_q1", "diff_lambda_k1", "diff_lambda_q2", "diff_lambda_k2")])
    par.append(np.broadcast_to(lam, (P, 256)))
    return dict(
        xT=f(x["x"][0].reshape(T, KD, P).transpose(2, 1, 0)), metaT=f(x["meta_tokens"].reshape(M, KD, P).transpose(2, 1, 0)),
        w1=f(w1), w2=f(w2), u=f(u), v=f(v), par=f(np.concatenate(par, axis=1)),
        positions=f(np.broadcast_to(x["positions_2"].astype(np.int32), (P, T))), **_constants())


def kernel(**inputs):
    import concourse.bacc as bacc
    from concourse.bass_utils import run_bass_kernel_spmd

    arrays = _layout({k: np.asarray(v) for k, v in inputs.items()})
    nc = bacc.Bacc("TRN2", target_bir_lowering=False, num_devices=1)
    a = {n: nc.dram_tensor(n, v.shape, mybir.dt.from_np(v.dtype), kind="ExternalInput").ap() for n, v in arrays.items()}
    a["gates"] = nc.dram_tensor("gates", (KEYS // 4, P, T // STAGE, 4 * STAGE), F32, kind="Internal").ap()
    a["early"] = nc.dram_tensor("early", (EARLY, P, T), F32, kind="Internal").ap()
    a["out"] = nc.dram_tensor("out", (P, KD, T), F32, kind="ExternalOutput").ap()
    build(nc, a)
    r = run_bass_kernel_spmd(nc, [arrays], core_ids=[0])
    return np.asarray(r.results[0]["out"]).transpose(2, 1, 0).reshape(1, T, D)
```
